# Optimizing a Trainium2 kernel written in Bass

```python
import jax, jax.numpy as jnp
from jax import lax
import numpy as np

D_MODEL = 1024
BATCH = 1
SEQ = 256
DEPTH = 2

CTX_LEN = 256
GRID_W = 64
HEAD_DIM = 64
N_HEADS = 8
N_KV_HEADS = 2
GQA = N_HEADS // N_KV_HEADS
ATTN_WIDTH = N_HEADS * HEAD_DIM
KV_WIDTH = N_KV_HEADS * HEAD_DIM
WINDOW = 128
ATTN_BLOCK = 128
ATTN_SCALE = HEAD_DIM ** -0.5
ROPE_BASE = 10000.0
CONV_WIDTH = D_MODEL // 4
GM_WIDTH = D_MODEL // 4
GM_GROUPS = 4
GM_HEAD = GM_WIDTH // GM_GROUPS
CHUNK = 128
MIX_WIDTH = ATTN_WIDTH + CONV_WIDTH + GM_WIDTH
IN_WIDTH = ATTN_WIDTH + 2 * KV_WIDTH + 3 * CONV_WIDTH + 2 * GM_WIDTH
SPLIT_POINTS = (ATTN_WIDTH,
                ATTN_WIDTH + KV_WIDTH,
                ATTN_WIDTH + 2 * KV_WIDTH,
                ATTN_WIDTH + 2 * KV_WIDTH + CONV_WIDTH,
                ATTN_WIDTH + 2 * KV_WIDTH + 2 * CONV_WIDTH,
                ATTN_WIDTH + 2 * KV_WIDTH + 3 * CONV_WIDTH,
                ATTN_WIDTH + 2 * KV_WIDTH + 3 * CONV_WIDTH + GM_WIDTH)
N_GROUPS = 4
EXP_PER_GROUP = 8
N_EXPERTS = N_GROUPS * EXP_PER_GROUP
TOP_K = 2
D_EXPERT = D_MODEL // 2
MOE_BLOCK = 128
ALPHA = (2 * DEPTH) ** 0.25
BETA = (8 * DEPTH) ** -0.25
LN_EPS = 1e-6
NEG_INF = -1e30


def layer_norm(x, g=None, b=None):
    xf = x.astype(jnp.float32)
    mu = jnp.mean(xf, axis=-1, keepdims=True)
    var = jnp.mean(jnp.square(xf - mu), axis=-1, keepdims=True)
    y = (xf - mu) * lax.rsqrt(var + LN_EPS)
    if g is not None:
        y = y * g.astype(jnp.float32) + b.astype(jnp.float32)
    return y.astype(x.dtype)

def _rope(x, pos):
    m = x.shape[-1] // 2
    freqs = ROPE_BASE ** (-jnp.arange(m, dtype=jnp.float32) / m)
    ang = pos.astype(jnp.float32)[:, None] * freqs[None, :]
    cos = jnp.cos(ang)[None, :, None, :]
    sin = jnp.sin(ang)[None, :, None, :]
    xf = x.astype(jnp.float32)
    a, b = xf[..., :m], xf[..., m:]
    return jnp.concatenate([a * cos - b * sin, b * cos + a * sin], axis=-1).astype(x.dtype)

def axial_rope(x, row, col):
    half = x.shape[-1] // 2
    return jnp.concatenate([_rope(x[..., :half], row), _rope(x[..., half:], col)], axis=-1)

def short_conv(u, w):
    up = jnp.pad(u, ((0, 0), (1, 1), (0, 0)))
    return up[:, :-2] * w[0] + up[:, 1:-1] * w[1] + up[:, 2:] * w[2]

def local_mixers(cb, cc, cx, gu, gv, conv_w, gm_ws, gm_bs):
    y_conv = cb * short_conv(cc * cx, conv_w)
    b_, l_ = gu.shape[:2]
    u = jax.nn.gelu(gu)
    v = layer_norm(jax.nn.gelu(gv)).reshape(b_, l_ // CHUNK, CHUNK, GM_GROUPS, GM_HEAD)
    s = jnp.einsum('gpq,bnqgc->bnpgc', gm_ws, v) + gm_bs.T[None, None, :, :, None]
    y_gm = u * s.reshape(b_, l_, GM_WIDTH).astype(u.dtype)
    return jnp.concatenate([y_conv, y_gm], axis=-1)

def sink_softmax(s, sink):
    col = jnp.broadcast_to(sink.astype(jnp.float32).reshape(N_KV_HEADS, GQA)[None, :, :, None, None],
                           s.shape[:-1] + (1,))
    return jax.nn.softmax(jnp.concatenate([col, s], axis=-1), axis=-1)[..., 1:]

def window_attention(q, k, v, k_ctx, v_ctx, sink):
    b_, s_ = q.shape[:2]
    nb = s_ // ATTN_BLOCK
    pad = ((0, 0), (ATTN_BLOCK, ATTN_BLOCK), (0, 0), (0, 0))
    kp, vp = jnp.pad(k, pad), jnp.pad(v, pad)
    span = 3 * ATTN_BLOCK
    rel = (jnp.arange(span)[None, :] - ATTN_BLOCK) - jnp.arange(ATTN_BLOCK)[:, None]
    band = jnp.abs(rel) <= WINDOW

    def one_block(n):
        start = n * ATTN_BLOCK
        qn = lax.dynamic_slice_in_dim(q, start, ATTN_BLOCK, axis=1).reshape(
            b_, ATTN_BLOCK, N_KV_HEADS, GQA, HEAD_DIM)
        kn = lax.dynamic_slice_in_dim(kp, start, span, axis=1)
        vn = lax.dynamic_slice_in_dim(vp, start, span, axis=1)
        kpos = start - ATTN_BLOCK + jnp.arange(span)
        valid = band & ((kpos >= 0) & (kpos < s_))[None, :]
        s_loc = jnp.einsum('bqkgd,bskd->bkgqs', qn, kn, preferred_element_type=jnp.float32) * ATTN_SCALE
        s_loc = jnp.where(valid, s_loc, NEG_INF)
        s_ctx = jnp.einsum('bqkgd,bckd->bkgqc', qn, k_ctx, preferred_element_type=jnp.float32) * ATTN_SCALE
        p = sink_softmax(jnp.concatenate([s_loc, s_ctx], axis=-1), sink).astype(v.dtype)
        o = (jnp.einsum('bkgqs,bskd->bqkgd', p[..., :span], vn)
             + jnp.einsum('bkgqc,bckd->bqkgd', p[..., span:], v_ctx))
        return o.reshape(b_, ATTN_BLOCK, ATTN_WIDTH)

    out = lax.map(one_block, jnp.arange(nb))
    return out.transpose(1, 0, 2, 3).reshape(b_, s_, ATTN_WIDTH)

def context_attention(q, k, v, sink):
    b_, c_ = q.shape[:2]
    qg = q.reshape(b_, c_, N_KV_HEADS, GQA, HEAD_DIM)
    s = jnp.einsum('bqkgd,bckd->bkgqc', qg, k, preferred_element_type=jnp.float32) * ATTN_SCALE
    p = sink_softmax(s, sink).astype(v.dtype)
    o = jnp.einsum('bkgqc,bckd->bqkgd', p, v)
    return o.reshape(b_, c_, ATTN_WIDTH)

def hier_moe(h, w_rg, b_rg, w_re, b_re, w1, w3, w2):
    n, d_ = h.shape
    hf = h.astype(jnp.float32)
    g_logit = hf @ w_rg.astype(jnp.float32) + b_rg.astype(jnp.float32)
    g_val, g_idx = lax.top_k(g_logit, 1)
    p_group = jnp.exp(g_val[:, 0] - jax.nn.logsumexp(g_logit, axis=-1))
    e_logit = (hf @ w_re.astype(jnp.float32)).reshape(n, N_GROUPS, EXP_PER_GROUP) \
        + b_re.astype(jnp.float32).reshape(N_GROUPS, EXP_PER_GROUP)
    e_logit = jnp.take_along_axis(e_logit, g_idx[:, :, None], axis=1)[:, 0]
    e_val, e_idx = lax.top_k(e_logit, TOP_K)
    gates = p_group[:, None] * jax.nn.softmax(e_val, axis=-1)
    expert = g_idx * EXP_PER_GROUP + e_idx

    a = n * TOP_K
    flat_e = expert.reshape(-1)
    flat_g = gates.reshape(-1)
    order = jnp.argsort(flat_e)
    se = flat_e[order]
    counts = jnp.bincount(flat_e, length=N_EXPERTS)
    starts = jnp.cumsum(counts) - counts
    padded = (counts + MOE_BLOCK - 1) // MOE_BLOCK * MOE_BLOCK
    pends = jnp.cumsum(padded)
    pstarts = pends - padded
    dest = pstarts[se] + jnp.arange(a) - starts[se]
    n_blocks = -(-a // MOE_BLOCK) + N_EXPERTS
    slot_tok = jnp.zeros(n_blocks * MOE_BLOCK, jnp.int32).at[dest].set((order // TOP_K).astype(jnp.int32))
    slot_gate = jnp.zeros(n_blocks * MOE_BLOCK, h.dtype).at[dest].set(flat_g[order].astype(h.dtype))
    block_e = jnp.minimum(jnp.searchsorted(pends, jnp.arange(n_blocks) * MOE_BLOCK, side='right'),
                          N_EXPERTS - 1)
    xs = h[slot_tok].reshape(n_blocks, MOE_BLOCK, d_)

    def run(args):
        xb, e = args
        return (jax.nn.silu(xb @ w1[e]) * (xb @ w3[e])) @ w2[e]

    ys = lax.map(run, (xs, block_e)).reshape(-1, d_)
    return jnp.zeros_like(h).at[slot_tok].add(ys * slot_gate[:, None])

def first_inputs(seed: int = 0) -> dict:
    key = jax.random.key(seed)
    ks = jax.random.split(key, 23)

    def nrm(k, shape, s):
        return jax.random.normal(k, shape, jnp.float32) * s

    d = D_MODEL
    return {
        'x': nrm(ks[0], (BATCH, SEQ, d), 1.0),
        'c': nrm(ks[1], (BATCH, d), 1.0),
        'ctx': nrm(ks[2], (BATCH, CTX_LEN, d), 1.0),
        'c_ctx': nrm(ks[3], (d,), 1.0),
        'w_ada': nrm(ks[4], (DEPTH, d, 6 * d), d ** -0.5),
        'b_ada': nrm(ks[5], (DEPTH, 6 * d), 0.02),
        'w_in': nrm(ks[6], (DEPTH, d, IN_WIDTH), d ** -0.5),
        'conv_w': nrm(ks[7], (DEPTH, 3, CONV_WIDTH), 3 ** -0.5),
        'attn_sink': nrm(ks[8], (DEPTH, N_HEADS), 0.5),
        'gm_ws': nrm(ks[9], (DEPTH, GM_GROUPS, CHUNK, CHUNK), CHUNK ** -0.5),
        'gm_bs': 1.0 + nrm(ks[10], (DEPTH, GM_GROUPS, CHUNK), 0.02),
        'w_out': nrm(ks[11], (DEPTH, MIX_WIDTH, d), BETA * MIX_WIDTH ** -0.5),
        'ln1_g': 1.0 + nrm(ks[12], (DEPTH, d), 0.02),
        'ln1_b': nrm(ks[13], (DEPTH, d), 0.02),
        'w_rg': nrm(ks[14], (DEPTH, d, N_GROUPS), d ** -0.5),
        'b_rg': nrm(ks[15], (DEPTH, N_GROUPS), 0.01),
        'w_re': nrm(ks[16], (DEPTH, d, N_EXPERTS), d ** -0.5),
        'b_re': nrm(ks[17], (DEPTH, N_EXPERTS), 0.01),
        'w1': nrm(ks[18], (DEPTH, N_EXPERTS, d, D_EXPERT), d ** -0.5),
        'w3': nrm(ks[19], (DEPTH, N_EXPERTS, d, D_EXPERT), d ** -0.5),
        'w2': nrm(ks[20], (DEPTH, N_EXPERTS, D_EXPERT, d), BETA * D_EXPERT ** -0.5),
        'ln2_g': 1.0 + nrm(ks[21], (DEPTH, d), 0.02),
        'ln2_b': nrm(ks[22], (DEPTH, d), 0.02),
    }

def first_block(x, c, ctx, c_ctx, w_ada, b_ada, w_in, conv_w, attn_sink, gm_ws, gm_bs, w_out,
              ln1_g, ln1_b, w_rg, b_rg, w_re, b_re, w1, w3, w2, ln2_g, ln2_b):
    b_, s_, d_ = x.shape
    c_len = ctx.shape[1]
    rows = s_ // GRID_W
    row = jnp.repeat(jnp.arange(rows), GRID_W)
    col = jnp.tile(jnp.arange(GRID_W), rows)
    c_act = jax.nn.silu(c)
    cc_act = jax.nn.silu(c_ctx)

    for l in range(DEPTH):
        last = l == DEPTH - 1
        mod_x = c_act @ w_ada[l] + b_ada[l]
        sh1, sc1, g1, sh2, sc2, g2 = jnp.split(mod_x[:, None, :], 6, axis=-1)
        n_mod = 2 if last else 6
        mod_c = (cc_act @ w_ada[l][:, :n_mod * d_] + b_ada[l][:n_mod * d_]).reshape(n_mod, d_)

        hx = x * (1 + sc1) + sh1
        hc = ctx * (1 + mod_c[1]) + mod_c[0]
        qx, kx, vx, cbx, ccx, cvx, gux, gvx = jnp.split(hx @ w_in[l], SPLIT_POINTS, axis=-1)
        qx = axial_rope(qx.reshape(b_, s_, N_HEADS, HEAD_DIM), row, col)
        kx = axial_rope(kx.reshape(b_, s_, N_KV_HEADS, HEAD_DIM), row, col)
        vx = vx.reshape(b_, s_, N_KV_HEADS, HEAD_DIM)
        if last:
            kc, vc = jnp.split(hc @ w_in[l][:, ATTN_WIDTH:ATTN_WIDTH + 2 * KV_WIDTH], 2, axis=-1)
        else:
            qc, kc, vc, cbc, ccc, cvc, guc, gvc = jnp.split(hc @ w_in[l], SPLIT_POINTS, axis=-1)
        kc = kc.reshape(b_, c_len, N_KV_HEADS, HEAD_DIM)
        vc = vc.reshape(b_, c_len, N_KV_HEADS, HEAD_DIM)

        att_x = window_attention(qx, kx, vx, kc, vc, attn_sink[l])
        o_x = jnp.concatenate(
            [att_x, local_mixers(cbx, ccx, cvx, gux, gvx, conv_w[l], gm_ws[l], gm_bs[l])], axis=-1) @ w_out[l]
        if not last:
            att_c = context_attention(qc, kc, vc, attn_sink[l])
            o_c = jnp.concatenate(
                [att_c, local_mixers(cbc, ccc, cvc, guc, gvc, conv_w[l], gm_ws[l], gm_bs[l])], axis=-1) @ w_out[l]
            ctx = layer_norm(ALPHA * ctx + mod_c[2] * o_c, ln1_g[l], ln1_b[l])
        x = layer_norm(ALPHA * x + g1 * o_x, ln1_g[l], ln1_b[l])

        hx = (x * (1 + sc2) + sh2).reshape(b_ * s_, d_)
        if last:
            tokens = hx
        else:
            hc = (ctx * (1 + mod_c[4]) + mod_c[3]).reshape(b_ * c_len, d_)
            tokens = jnp.concatenate([hx, hc], axis=0)
        y = hier_moe(tokens, w_rg[l], b_rg[l], w_re[l], b_re[l], w1[l], w3[l], w2[l])
        if not last:
            ctx = layer_norm(ALPHA * ctx + mod_c[5] * y[b_ * s_:].reshape(b_, c_len, d_), ln2_g[l], ln2_b[l])
        x = layer_norm(ALPHA * x + g2 * y[:b_ * s_].reshape(b_, s_, d_), ln2_g[l], ln2_b[l])

    return x


MIX_WIDTH_2 = 2 * D_MODEL
BLOCK = 128
SWA_HEADS = (MIX_WIDTH_2 // 4) // HEAD_DIM
SWA_KV_HEADS = SWA_HEADS // 4
SWA_WINDOW = 128
FOX_HEADS = (MIX_WIDTH_2 // 4) // HEAD_DIM
SSM_HEAD_DIM = 64
SSM_HEADS = (MIX_WIDTH_2 // 2) // SSM_HEAD_DIM
SSM_GROUPS = 2
SSM_STATE = 128
SSM_CONV = 4
SSM_CHUNK = 128
MEM_TOKENS = 256
MEM_HEADS = 4
MEM_HEAD_DIM = D_MODEL // MEM_HEADS
ROPE_THETA = 10000.0
EPS = 1e-6
NEG_INF_2 = -1e30

SWA_W = SWA_HEADS * HEAD_DIM
SWA_KV_W = SWA_KV_HEADS * HEAD_DIM
FOX_W = FOX_HEADS * HEAD_DIM
SSM_W = SSM_HEADS * SSM_HEAD_DIM
SSM_BC_W = SSM_GROUPS * SSM_STATE
SSM_CONV_W = SSM_W + 2 * SSM_BC_W
IN_SPLITS = (SWA_W, SWA_KV_W, SWA_KV_W, SWA_W,
             FOX_W, FOX_W, FOX_W, FOX_HEADS, FOX_W,
             SSM_W, SSM_CONV_W, SSM_HEADS)
IN_W = SWA_W + 2 * SWA_KV_W + SWA_W + 4 * FOX_W + FOX_HEADS + SSM_W + SSM_CONV_W + SSM_HEADS


def _offsets(sizes):
    out, acc = [], 0
    for s in sizes[:-1]:
        acc += s
        out.append(acc)
    return out

def rms_norm(x, w):
    xf = x.astype(jnp.float32)
    y = xf * lax.rsqrt(jnp.mean(xf * xf, axis=-1, keepdims=True) + EPS)
    return (y * w.astype(jnp.float32)).astype(x.dtype)

def rope_tables(seq):
    pos = jnp.arange(seq, dtype=jnp.float32)
    inv = 1.0 / (ROPE_THETA ** (jnp.arange(0, HEAD_DIM, 2, dtype=jnp.float32) / HEAD_DIM))
    ang = pos[:, None] * inv[None, :]
    return jnp.cos(ang), jnp.sin(ang)

def apply_rope(x, cos, sin):
    xf = x.astype(jnp.float32)
    x1, x2 = jnp.split(xf, 2, axis=-1)
    c = cos[None, :, None, :]
    s = sin[None, :, None, :]
    return jnp.concatenate([x1 * c - x2 * s, x2 * c + x1 * s], axis=-1).astype(x.dtype)

def sliding_window_attention(q, k, v, sinks):
    b, s, hq, hd = q.shape
    hkv = k.shape[2]
    g = hq // hkv
    n = s // BLOCK
    qb = q.reshape(b, n, BLOCK, hkv, g, hd)
    kb = k.reshape(b, n, BLOCK, hkv, hd)
    vb = v.reshape(b, n, BLOCK, hkv, hd)
    pad = ((0, 0), (1, 0), (0, 0), (0, 0), (0, 0))
    kcat = jnp.concatenate([jnp.pad(kb, pad)[:, :-1], kb], axis=2)
    vcat = jnp.concatenate([jnp.pad(vb, pad)[:, :-1], vb], axis=2)
    scores = jnp.einsum('bnqkgd,bnskd->bnkgqs', qb, kcat).astype(jnp.float32) * (hd ** -0.5)
    qi = jnp.arange(BLOCK)[:, None]
    si = jnp.arange(2 * BLOCK)[None, :] - BLOCK
    rel = qi - si
    band = (rel >= 0) & (rel < SWA_WINDOW)
    valid = (jnp.arange(n)[:, None, None] * BLOCK + si[None]) >= 0
    mask = band[None] & valid
    scores = jnp.where(mask[None, :, None, None], scores, NEG_INF_2)
    sink = sinks.astype(jnp.float32).reshape(hkv, g)[None, None, :, :, None, None]
    m = jnp.maximum(jnp.max(scores, axis=-1, keepdims=True), sink)
    p = jnp.exp(scores - m)
    probs = (p / (jnp.sum(p, axis=-1, keepdims=True) + jnp.exp(sink - m))).astype(v.dtype)
    out = jnp.einsum('bnkgqs,bnskd->bnqkgd', probs, vcat)
    return out.reshape(b, s, hq, hd)

def forgetting_attention(q, k, v, log_f):
    b, s, h, hd = q.shape
    n = s // BLOCK
    c = jnp.cumsum(log_f, axis=1).transpose(0, 2, 1)
    qb = q.reshape(b, n, BLOCK, h, hd).swapaxes(0, 1)
    cq = c.reshape(b, h, n, BLOCK).transpose(2, 0, 1, 3)
    kpos = jnp.arange(s)
    scale = hd ** -0.5

    def one_block(args):
        qi, ci, i = args
        logits = jnp.einsum('bqhd,bkhd->bhqk', qi, k).astype(jnp.float32) * scale
        logits = logits + ci[..., :, None] - c[:, :, None, :]
        qpos = i * BLOCK + jnp.arange(BLOCK)
        mask = kpos[None, :] <= qpos[:, None]
        logits = jnp.where(mask, logits, NEG_INF_2)
        probs = jax.nn.softmax(logits, axis=-1).astype(v.dtype)
        return jnp.einsum('bhqk,bkhd->bqhd', probs, v)

    out = lax.map(one_block, (qb, cq, jnp.arange(n)))
    return out.swapaxes(0, 1).reshape(b, s, h, hd)

def causal_depthwise_conv(u, w, bias):
    kw = w.astype(u.dtype)[:, None, :]
    out = lax.conv_general_dilated(u, kw, window_strides=(1,), padding=[(SSM_CONV - 1, 0)],
                                   dimension_numbers=('NWC', 'WIO', 'NWC'),
                                   feature_group_count=u.shape[-1])
    return out + bias.astype(u.dtype)

def ssd_chunked(x, dt, a, bmat, cmat):
    b, s, h, p = x.shape
    g, nst = bmat.shape[2], bmat.shape[3]
    hg = h // g
    L = SSM_CHUNK
    nc = s // L
    xs = (x.astype(jnp.float32) * dt[..., None]).reshape(b, nc, L, g, hg, p)
    acs = jnp.cumsum((dt * a.astype(jnp.float32)).reshape(b, nc, L, g, hg), axis=2)
    bm = bmat.astype(jnp.float32).reshape(b, nc, L, g, nst)
    cm = cmat.astype(jnp.float32).reshape(b, nc, L, g, nst)
    diff = acs[:, :, :, None] - acs[:, :, None, :]
    causal = jnp.tril(jnp.ones((L, L), dtype=bool))
    decay = jnp.exp(jnp.where(causal[:, :, None, None], diff, NEG_INF_2))
    cb = jnp.einsum('bclgn,bcsgn->bclsg', cm, bm)
    y_diag = jnp.einsum('bclsg,bclsgh,bcsghp->bclghp', cb, decay, xs)
    decay_st = jnp.exp(acs[:, :, -1:] - acs)
    states = jnp.einsum('bclgn,bclgh,bclghp->bcghpn', bm, decay_st, xs)
    chunk_decay = jnp.exp(acs[:, :, -1])

    def step(carry, inp):
        st, dec = inp
        return carry * dec[..., None, None] + st, carry

    init = jnp.zeros((b, g, hg, p, nst), jnp.float32)
    _, prev = lax.scan(step, init, (states.swapaxes(0, 1), chunk_decay.swapaxes(0, 1)))
    prev = prev.swapaxes(0, 1)
    y_off = jnp.einsum('bclgn,bcghpn,bclgh->bclghp', cm, prev, jnp.exp(acs))
    return (y_diag + y_off).reshape(b, s, h, p)

def hybrid_mixer(h, w_in, b_forget, sinks, conv_w, conv_b, dt_bias, a_log, d_skip,
                 ssm_norm_w, w_out, cos, sin):
    b, s, _ = h.shape
    proj = h @ w_in.astype(h.dtype)
    (q_a, k_a, v_a, g_a, q_b, k_b, v_b, f_b, g_b, z_c, xbc_c, dt_c) = jnp.split(
        proj, _offsets(IN_SPLITS), axis=-1)
    qa = apply_rope(q_a.reshape(b, s, SWA_HEADS, HEAD_DIM), cos, sin)
    ka = apply_rope(k_a.reshape(b, s, SWA_KV_HEADS, HEAD_DIM), cos, sin)
    va = v_a.reshape(b, s, SWA_KV_HEADS, HEAD_DIM)
    ya = sliding_window_attention(qa, ka, va, sinks).reshape(b, s, SWA_W)
    ya = ya * jax.nn.silu(g_a)
    log_f = jax.nn.log_sigmoid(f_b.astype(jnp.float32) + b_forget.astype(jnp.float32))
    yb = forgetting_attention(q_b.reshape(b, s, FOX_HEADS, HEAD_DIM),
                              k_b.reshape(b, s, FOX_HEADS, HEAD_DIM),
                              v_b.reshape(b, s, FOX_HEADS, HEAD_DIM), log_f).reshape(b, s, FOX_W)
    yb = yb * jax.nn.silu(g_b)
    xbc = jax.nn.silu(causal_depthwise_conv(xbc_c, conv_w, conv_b))
    xs, bm, cm = jnp.split(xbc, [SSM_W, SSM_W + SSM_BC_W], axis=-1)
    xs = xs.reshape(b, s, SSM_HEADS, SSM_HEAD_DIM)
    bm = bm.reshape(b, s, SSM_GROUPS, SSM_STATE)
    cm = cm.reshape(b, s, SSM_GROUPS, SSM_STATE)
    dt = jax.nn.softplus(dt_c.astype(jnp.float32) + dt_bias.astype(jnp.float32))
    a = -jnp.exp(a_log.astype(jnp.float32))
    yc = ssd_chunked(xs, dt, a, bm, cm) + d_skip.astype(jnp.float32)[:, None] * xs.astype(jnp.float32)
    yc = yc.reshape(b, s, SSM_W).astype(h.dtype)
    yc = rms_norm(yc * jax.nn.silu(z_c), ssm_norm_w)
    y = jnp.concatenate([ya, yb, yc], axis=-1)
    return y @ w_out.astype(h.dtype)

def memory_cross_attention(h, mem_n, wq, wk, wv, wo):
    b, s, _ = h.shape
    m = mem_n.shape[1]
    q = (h @ wq.astype(h.dtype)).reshape(b, s, MEM_HEADS, MEM_HEAD_DIM)
    k = (mem_n @ wk.astype(h.dtype)).reshape(b, m, MEM_HEADS, MEM_HEAD_DIM)
    v = (mem_n @ wv.astype(h.dtype)).reshape(b, m, MEM_HEADS, MEM_HEAD_DIM)
    logits = jnp.einsum('bqhd,bkhd->bhqk', q, k).astype(jnp.float32) * (MEM_HEAD_DIM ** -0.5)
    probs = jax.nn.softmax(logits, axis=-1).astype(v.dtype)
    out = jnp.einsum('bhqk,bkhd->bqhd', probs, v).reshape(b, s, D_MODEL)
    return out @ wo.astype(h.dtype)

def second_inputs(seed: int = 0) -> dict:
    key = jax.random.key(seed)
    ks = jax.random.split(key, 20)
    f32 = jnp.float32

    def nrm(k, shape, scale):
        return jax.random.normal(k, shape, f32) * scale

    dt0 = jnp.exp(jax.random.uniform(ks[7], (DEPTH, SSM_HEADS), f32, np.log(1e-3), np.log(1e-1)))
    return {
        "x": nrm(ks[0], (BATCH, SEQ, D_MODEL), 1.0),
        "mem": nrm(ks[1], (BATCH, MEM_TOKENS, D_MODEL), 1.0),
        "norm_mix_w": 1.0 + nrm(ks[2], (DEPTH, D_MODEL), 0.02),
        "w_in": nrm(ks[3], (DEPTH, D_MODEL, IN_W), D_MODEL ** -0.5),
        "b_forget": jax.random.uniform(ks[4], (DEPTH, FOX_HEADS), f32, 1.0, 6.0),
        "swa_sinks": nrm(ks[5], (DEPTH, SWA_HEADS), 0.5),
        "conv_w": nrm(ks[6], (DEPTH, SSM_CONV, SSM_CONV_W), SSM_CONV ** -0.5),
        "conv_b": nrm(ks[8], (DEPTH, SSM_CONV_W), 0.02),
        "dt_bias": dt0 + jnp.log(-jnp.expm1(-dt0)),
        "a_log": jnp.log(jax.random.uniform(ks[9], (DEPTH, SSM_HEADS), f32, 1.0, 16.0)),
        "d_skip": 1.0 + nrm(ks[10], (DEPTH, SSM_HEADS), 0.1),
        "ssm_norm_w": 1.0 + nrm(ks[11], (DEPTH, SSM_W), 0.02),
        "w_out": nrm(ks[12], (DEPTH, MIX_WIDTH_2, D_MODEL), MIX_WIDTH_2 ** -0.5),
        "norm_xq_w": 1.0 + nrm(ks[13], (DEPTH, D_MODEL), 0.02),
        "norm_mem_w": 1.0 + nrm(ks[14], (DEPTH, D_MODEL), 0.02),
        "w_mq": nrm(ks[15], (DEPTH, D_MODEL, D_MODEL), D_MODEL ** -0.5),
        "w_mk": nrm(ks[16], (DEPTH, D_MODEL, D_MODEL), D_MODEL ** -0.5),
        "w_mv": nrm(ks[17], (DEPTH, D_MODEL, D_MODEL), D_MODEL ** -0.5),
        "w_mo": nrm(ks[18], (DEPTH, D_MODEL, D_MODEL), D_MODEL ** -0.5),
        "final_norm_w": 1.0 + nrm(ks[19], (D_MODEL,), 0.02),
    }

def second_block(x, mem, norm_mix_w, w_in, b_forget, swa_sinks, conv_w, conv_b, dt_bias, a_log,
              d_skip, ssm_norm_w, w_out, norm_xq_w, norm_mem_w, w_mq, w_mk, w_mv, w_mo,
              final_norm_w):
    cos, sin = rope_tables(x.shape[1])
    for l in range(DEPTH):
        h = rms_norm(x, norm_mix_w[l])
        x = x + hybrid_mixer(h, w_in[l], b_forget[l], swa_sinks[l], conv_w[l], conv_b[l],
                             dt_bias[l], a_log[l], d_skip[l], ssm_norm_w[l], w_out[l], cos, sin)
        hq = rms_norm(x, norm_xq_w[l])
        mem_n = rms_norm(mem, norm_mem_w[l])
        x = x + memory_cross_attention(hq, mem_n, w_mq[l], w_mk[l], w_mv[l], w_mo[l])
    return rms_norm(x, final_norm_w)


def setup_inputs(seed=0):
    out = dict(first_inputs(seed))
    for name, value in second_inputs(seed + 1).items():
        if name != "x":
            out[name + "_2"] = value
    return out


def reference(
    x, c, ctx, c_ctx, w_ada, b_ada, w_in, conv_w, attn_sink, gm_ws, gm_bs, w_out, ln1_g, ln1_b,
    w_rg, b_rg, w_re, b_re, w1, w3, w2, ln2_g, ln2_b, mem_2, norm_mix_w_2, w_in_2, b_forget_2,
    swa_sinks_2, conv_w_2, conv_b_2, dt_bias_2, a_log_2, d_skip_2, ssm_norm_w_2, w_out_2,
    norm_xq_w_2, norm_mem_w_2, w_mq_2, w_mk_2, w_mv_2, w_mo_2, final_norm_w_2,
):
    x = first_block(
        x, c, ctx, c_ctx, w_ada, b_ada, w_in, conv_w, attn_sink, gm_ws, gm_bs, w_out, ln1_g,
        ln1_b, w_rg, b_rg, w_re, b_re, w1, w3, w2, ln2_g, ln2_b,
    )
    return second_block(
        x, mem_2, norm_mix_w_2, w_in_2, b_forget_2, swa_sinks_2, conv_w_2, conv_b_2, dt_bias_2,
        a_log_2, d_skip_2, ssm_norm_w_2, w_out_2, norm_xq_w_2, norm_mem_w_2, w_mq_2, w_mk_2,
        w_mv_2, w_mo_2, final_norm_w_2,
    )


_drawn_inputs = setup_inputs


def setup_inputs(seed=0):
    import zlib

    import numpy as np

    out = dict(_drawn_inputs(seed))
    spreads = {}
    factors = {'attn_sink': 8.0,
     'gm_bs': 5.396,
     'b_rg': 6.98,
     'b_re': 3.906,
     'swa_sinks_2': 8.0,
     'ssm_norm_w_2': 3.565,
     'norm_xq_w_2': 8.0,
     'norm_mem_w_2': 8.0}
    for name, (base, spread) in spreads.items():
        noise = np.random.default_rng([zlib.crc32(name.encode()), seed]).standard_normal(out[name].shape)
        drawn = base * np.exp(spread * noise) if base else spread * noise
        out[name] = __import__('jax').numpy.asarray(drawn.astype(out[name].dtype))
    for name, factor in factors.items():
        out[name] = (out[name] * factor).astype(out[name].dtype)
    return out
```

```python
from collections import defaultdict
from contextlib import ExitStack

import numpy as np

import concourse.bass as bass
from concourse import mybir

F32 = mybir.dt.float32
I32 = mybir.dt.int32
ALU = mybir.AluOpType
ACT = mybir.ActivationFunctionType
AX = mybir.AxisListType.X

P = 128
D = 1024
DC = D // P
DEPTH = 2
NX = 2
NH, HD, NKV = 8, 64, 2
GQA = NH // NKV
E = 32
NG, EPG = 4, 8
ALPHA = (2 * DEPTH) ** 0.25
EPS = 1e-6
QSCALE = HD ** -0.5
MEM_QSCALE = 256 ** -0.5
RING = 4
TILE = DC * 512
UNROLL = 4
OVERFLOW = tuple((2 * n - 1) // (P + 1) for n in (4 * P, 2 * P))
ADA_TILES, IN_TILES, OUT_TILES = 12, 4, 2
IN2_TILES, OUT2_TILES, MEM_TILES = 12, 4, 8

_C = {}
_o = 0
for _n, _w in (("ident", 128), ("ustrict", 128), ("z0", 128), ("uincl", 128), ("ones", 128),
               ("z1", 128), ("causal", 128), ("none", 128), ("ge", 128), ("z2", 128),
               ("gt", 128), ("causal2", 128), ("iota", 128), ("tokid", 4), ("ropeA", 256),
               ("ropeB", 256)):
    _C[_n] = _o
    _o += _w
CONST_W = _o


def constants():
    c = np.zeros((P, CONST_W), np.float32)
    i = np.arange(P)[:, None]
    j = np.arange(P)[None, :]
    neg = np.float32(-1e30)

    def put(name, v):
        v = np.asarray(v, np.float32)
        c[:, _C[name]:_C[name] + v.shape[1]] = v

    put("ident", i == j)
    put("ustrict", i < j)
    put("uincl", i <= j)
    put("ones", np.ones((P, P)))
    put("causal", np.where(j <= i, 0, neg))
    put("causal2", np.where(j <= i, 0, neg))
    put("none", np.full((P, P), neg))
    put("ge", np.where(j >= i, 0, neg))
    put("gt", np.where(j > i, 0, neg))
    put("iota", np.broadcast_to(j, (P, P)))
    put("tokid", np.arange(4)[None, :] * P + np.arange(P)[:, None])
    for t in range(NX):
        pos = np.arange(P) + t * P
        fr = (np.float32(10000.0) ** (-np.arange(16, dtype=np.float32) / np.float32(16)))
        row = (pos // 64).astype(np.float32)[:, None] * fr
        col = (pos % 64).astype(np.float32)[:, None] * fr
        cos = np.concatenate([np.cos(row)] * 2 + [np.cos(col)] * 2, 1)
        sin = np.concatenate([-np.sin(row), np.sin(row), -np.sin(col), np.sin(col)], 1)
        o = _C["ropeA"] + t * 128
        c[:, o:o + 64], c[:, o + 64:o + 128] = cos, sin
        inv = np.float32(1.0) / (np.float32(10000.0) ** (np.arange(0, 64, 2, dtype=np.float32) / np.float32(64)))
        ang = pos.astype(np.float32)[:, None] * inv
        o = _C["ropeB"] + t * 128
        c[:, o:o + 64] = np.concatenate([np.cos(ang)] * 2, 1)
        c[:, o + 64:o + 128] = np.concatenate([-np.sin(ang), np.sin(ang)], 1)
    return c


def build(nc, d):
    with ExitStack() as ctx:
        program(nc, d, ctx)


def program(nc, d, ctx):
    def sb(name, shape, dt=F32):
        return ctx.enter_context(nc.sbuf_tensor(name, shape, dt))

    def sem(name):
        return ctx.enter_context(nc.semaphore(name))

    cst = sb("cst", [P, CONST_W])
    ring = sb("ring", [P, RING, DC, 512])
    S = sb("S", [P, 4, D])
    hb = sb("hb", [P, 4, D])
    hT = sb("hT", [P, 4 * D])
    modB = sb("modB", [P, 4, D])
    lnB = sb("lnB", [P, 2, D])
    small = sb("small", [P, 1024])
    cact = sb("cact", [P, DC, 2])
    slot_tok = sb("slot_tok", [P, E + OVERFLOW[0]], I32)
    dest = sb("dest", [P, 4, 2, 2], I32)
    wide = sb("wide", [P, E], I32)
    gates = sb("gates", [P, 2, 4])
    ovid = sb("ovid", [P, 9], I32)
    idcol = sb("idcol", [P, 2], I32)
    SCR = 14900
    scr = sb("scr", [P, SCR])
    ps = ctx.enter_context(nc.psum_tensor("ps", [P, 8, 512], F32))

    def const(name, w=P, off=0):
        return cst[:, _C[name] + off:_C[name] + off + w]

    ident = const("ident")
    iota = const("iota")

    class Carve:

        def __init__(self, start=0):
            self.at = start

        def __call__(self, *shape):
            n = int(np.prod(shape))
            v = scr[:, self.at:self.at + n]
            self.at += n
            assert self.at <= SCR, self.at
            if len(shape) == 2:
                v = v.rearrange("p (a b) -> p a b", a=shape[0])
            if len(shape) == 3:
                v = v.rearrange("p (a b c) -> p a b c", a=shape[0], b=shape[1])
            return v

    hT8 = hT[:, :].rearrange("p (c t) -> p c t", c=DC)
    hT16 = hT[:, :].rearrange("p (c t) -> p c t", c=16)

    cv = Carve()
    sbuf_s = cv(2, 512)
    sbuf_p = cv(2, 512)
    sbuf_pT = cv(2, 4, 128)
    attn_end = cv.at
    cv = Carve(attn_end)
    ropet = cv(512)
    vA = cv(4, 128)
    guv = cv(4, 512)
    qTA = cv(4, 512)
    kTA = cv(2, 512)
    cbT = cv(2, 512)
    ccT = cv(512)
    uT = cv(2, 2, 258)
    gmw = cv(4, 128)
    cact32 = cv(DC, 32)
    mst = cv(ADA_TILES, P)
    cv = Carve()
    xg = cv(2, D)
    xgT = cv(2, DC, 128)
    eb = cv(2, 512)
    gbuf = cv(2, 512)
    gT = cv(2, 4, 128)
    ysb = cv(2, D)
    wr = cv(DC, 36)
    rb = cv(36)
    cv = Carve()
    lg = cv(4, 36)
    em = cv(4, 32)
    oh = [cv(4, 32), cv(4, 32)]
    t32 = [cv(4, 32), cv(4, 32)]
    mem_ = cv(4, 32)
    rk = cv(160)
    nov = cv(32)
    sc0 = cv(32)
    sc1 = cv(32)
    ovx = cv(32)
    nar = cv(32)
    bo = [cv(4, 41), cv(4, 41)]
    R = [cv(4, 128), cv(4, 128)]
    ov3 = cv(8, 32)
    ov4 = cv(8, 32)
    idxf = cv(41)
    cv = Carve()
    yg = [cv(2, D), cv(2, D)]
    cv = Carve(attn_end)
    ropeu = cv(512)
    vaB = cv(2, 128)
    vbB = cv(2, 512)
    qaT = cv(4, 256)
    kaT = cv(2, 256)
    qbT = cv(4, 256)
    kbT = cv(4, 256)
    xsn = scr[:, cv.at - 2048:cv.at].rearrange("p (a b) -> p a b", a=2)
    xp = cv(12, 259)
    xc = cv(12, 256)
    bmn = cv(256)
    cv = Carve(attn_end)
    qmT = cv(8, 256)
    kmT = cv(8, 256)
    vm = cv(2, D)
    memn = cv(2, D)
    xpf = xp.rearrange("p a b -> p (a b)")
    xdt = xpf[:, 0:2048].rearrange("p (a b) -> p a b", a=2)
    xds = xpf[:, 2048:3072]
    W = sbuf_s
    W2 = sbuf_p
    cbm = sbuf_pT.rearrange("p a b c -> p (a b c)")[:, 0:512].rearrange("p (t g l) -> p t g l", t=2, g=2)
    stT = qaT.rearrange("p a b -> p (a b)").rearrange("p (g x) -> p g x", g=2)
    zB = modB[:, 0:2, :]
    gaB = modB[:, 2, :].rearrange("p (t x) -> p t x", t=2)
    gbB = modB[:, 3, :].rearrange("p (t x) -> p t x", t=2)
    mixB = hb[:, :, :].rearrange("p a b -> p (a b)").rearrange("p (t x) -> p t x", t=2)
    hB = S[:, 2:4, :]

    class Cols:
        def __init__(self):
            self.at = 0

        def __call__(self, n):
            v = small[:, self.at:self.at + n]
            self.at += n
            assert self.at <= 1024
            return v

    col = Cols()
    nm = col(32).rearrange("p (t h) -> p t h", t=4)
    rsum = col(32).rearrange("p (t h) -> p t h", t=4)
    rinv = col(32).rearrange("p (t h) -> p t h", t=4)
    mx = col(2)
    snk = col(8)
    esk = col(8)
    bst = col(12)
    mv = col(8).rearrange("p (t x) -> p t x", t=4)
    rstd = col(4)
    gmb = col(4)
    cwA = col(6).rearrange("p (c k) -> p c k", c=2)
    rt = [col(4) for _ in range(12)]
    g4 = [col(16).rearrange("p (t g) -> p t g", t=4) for _ in range(3)]
    fbd = col(48).rearrange("p (t x) -> p t x", t=2)
    bfd = col(24)
    sp = [col(48).rearrange("p (t x) -> p t x", t=2) for _ in range(4)]
    aneg = col(16)
    dskip = col(16)
    dta = col(32).rearrange("p (t x) -> p t x", t=2)
    cs = col(80)
    eacs = col(16)
    dst = col(16)
    cwB = col(48).rearrange("p (c k) -> p c k", c=12)
    cbB = col(12)
    ce = col(16).rearrange("p (c x) -> p c x", c=8)
    ov1 = col(8)

    mod_d = nc.dram_tensor("mod_scratch", (DEPTH, 2, 6 * D), F32, kind="Internal").ap()
    tok_d = nc.dram_tensor("tok_scratch", (512, D), F32, kind="Internal").ap()
    ys_d = nc.dram_tensor("ys_scratch", ((E + OVERFLOW[0]) * P, D), F32, kind="Internal").ap()

    ring_full = [sem(f"ring_full{i}") for i in range(RING)]
    acc_full, acc_free = sem("acc_full"), sem("acc_free")
    tp_full, tp_free = sem("tp_full"), sem("tp_free")
    sc_full, sc_free = sem("sc_full"), sem("sc_free")
    dve_step = sem("dve_step")
    const_in = sem("const_in")
    par_in = sem("par_in")
    bada_in = sem("bada_in")
    rows_out = sem("rows_out")
    mod_in = sem("mod_in")
    rows_ready = sem("rows_ready")
    mod_used = sem("mod_used")
    c_exp, c_ready = sem("c_exp"), sem("c_ready")
    h_ready = sem("h_ready")
    qk_ready = sem("qk_ready")
    nm_ready = sem("nm_ready")
    p_ready = sem("p_ready")
    dve_to_act = sem("dve_to_act")
    act_to_dve = sem("act_to_dve")
    v_ready = sem("v_ready")
    w_ready = sem("w_ready")
    tok_out = sem("tok_out")
    idx_ready = sem("idx_ready")
    tok_ready = sem("tok_ready")
    comb_in = [sem("comb_in0"), sem("comb_in1")]
    comb_used = sem("comb_used")
    phase = sem("phase")
    out_ready, out_done = sem("out_ready"), sem("out_done")
    m_xg = [sem("m_xg0"), sem("m_xg1")]
    m_xt, m_xe = sem("m_xt"), sem("m_xe")
    m_h1, m_h3 = sem("m_h1"), sem("m_h3")
    m_e = sem("m_e")
    m_g = sem("m_g")
    m_gt, m_ge = sem("m_gt"), sem("m_ge")
    m_y, m_ye = sem("m_y"), sem("m_ye")
    m_yw = [sem("m_yw0"), sem("m_yw1")]
    pool_step = sem("pool_step")
    ys_init = sem("ys_init")
    ov = [{n: sem(f"ov{l}_{n}") for n in ("w1_in", "w3_in", "w2_in", "ids", "rows_in", "turned", "rows_T", "h13",
                                          "silu", "gated", "gated_turned", "gated_T", "y", "y_copied", "y_out")}
          for l in range(DEPTH)]

    def acc(n):
        return ps[:, n % 4, :]

    def tpb(n):
        return ps[:, 4 + n % 2, :]

    def scb(n):
        return ps[:, 6 + n % 2, :]

    SEG_A = ADA_TILES + IN_TILES + OUT_TILES
    SEG_B = IN2_TILES + OUT2_TILES + MEM_TILES
    baseA, baseM, baseB = [], [], []
    g = 0
    for l in range(DEPTH):
        baseA.append(g)
        g += SEG_A
        baseM.append(g)
        g += 3 * E
    for l in range(DEPTH):
        baseB.append(g)
        g += SEG_B
    blocks_before = [0, E]
    gathers_before = [0, E + 1]
    gpar_before = [(0, 0), (E // 2 + 1, E // 2)]
    released = {}
    for l in range(DEPTH):
        for b in range(E):
            for k, s in enumerate((m_h1, m_h3, m_y)):
                released[baseM[l] + 3 * b + k] = (s, blocks_before[l] + b + 1)

    def par_a(l, k):
        return 16 * (10 * l + k)

    def par_b(l, k):
        return 16 * (20 + 12 * l + k)

    block = ctx.enter_context(nc.Block())

    @block.tensor
    def _(pe):
        T = defaultdict(int)
        mm = nc.tensor.matmul

        def acc_bank():
            if T["acc"] >= 4:
                pe.wait_ge(acc_free, T["acc"] - 3)
            T["acc"] += 1
            return acc(T["acc"] - 1)

        def tp_bank():
            if T["tp"] >= 2:
                pe.wait_ge(tp_free, T["tp"] - 1)
            T["tp"] += 1
            return tpb(T["tp"] - 1)

        def sc_bank():
            if T["sc"] >= 2:
                pe.wait_ge(sc_free, T["sc"] - 1)
            T["sc"] += 1
            return scb(T["sc"] - 1)

        def tile(g):
            pe.wait_ge(ring_full[g % RING], 16 * (g // RING + 1))
            return ring[:, g % RING, :, :]

        def release(g):
            released[g] = (acc_free, T["acc"])

        def need(name, s, n=1):
            T[name] += n
            pe.wait_ge(s, T[name])

        def turn(chunks):
            bank = tp_bank()
            for i, c in enumerate(chunks):
                last = nc.tensor.transpose(bank[:, i * P:(i + 1) * P], c, ident)
            last.then_inc(tp_full, 1)

        def turn_rows(t, src, n):
            for c in range(0, n, 4):
                turn([src[:, (c + i) * P:(c + i + 1) * P] for i in range(min(4, n - c))])

        def rows_times(lhs, w, cols, n=DC):
            bank = acc_bank()
            for c in range(n):
                last = mm(bank[:, 0:cols], lhs(c), w(c), start=(c == 0), stop=(c == n - 1))
            last.then_inc(acc_full, 1)

        def attention(units, score, values, nkc, hw):
            per = 512 // hw
            for i in range(min(2, len(units))):
                score(*units[i])
            bank = None
            for i, (n, h) in enumerate(units):
                need("p", p_ready)
                turn([sbuf_p[:, i % 2, k * P:(k + 1) * P] for k in range(nkc)])
                if i + 2 < len(units):
                    score(*units[i + 2])
                pe.wait_ge(tp_free, T["tp"])
                if h % per == 0:
                    bank = acc_bank()
                o = (h % per) * hw
                for k in range(nkc):
                    last = mm(bank[:, o:o + hw], sbuf_pT[:, i % 2, k, :], values(n, h, k),
                              start=(k == 0), stop=(k == nkc - 1))
                if h % per == per - 1:
                    last.then_inc(acc_full, 1)

        def gqa_score(qT, kT, lo, hi):
            def score(n, h):
                bank = sc_bank()
                o = HD * (h % 2)
                mm(bank[:, 0:hi(n) - lo(n)], qT[o:o + HD, h // 2, n * P:(n + 1) * P],
                   kT[o:o + HD, h // GQA, lo(n):hi(n)], start=True, stop=True).then_inc(sc_full, 1)
            return score

        pe.wait_ge(const_in, 16 * 3)
        for l in range(DEPTH):
            g = baseA[l]
            nt = 4 if l < DEPTH - 1 else NX
            if l == 0:
                pe.wait_ge(c_ready, 1)
            for j in range(ADA_TILES):
                w = tile(g)
                bank = acc_bank()
                for c in range(DC):
                    for q in range(4):
                        last = mm(bank[32 * q:32 * q + 32, 0:P], cact32[:, c, :], w[:, c, q * P:(q + 1) * P],
                                  start=(c == 0), stop=(c == DC - 1))
                last.then_inc(acc_full, 1)
                release(g)
                g += 1
            for t in range(4):
                need("h", h_ready)
                turn_rows(t, hb[:, t, :], DC)
            pe.wait_ge(tp_free, T["tp"])
            w = tile(g)
            for t in range(nt):
                rows_times(lambda c: hT8[:, c, t * P:(t + 1) * P], lambda c: w[:, c, :], 512)
            release(g)
            g += 1
            w = tile(g)
            for t in range(4):
                cols = 512 if t < nt else 256
                rows_times(lambda c: hT8[:, c, t * P:(t + 1) * P], lambda c: w[:, c, 0:cols], cols)
            release(g)
            g += 1
            w = tile(g)
            for t in range(nt):
                rows_times(lambda c: hT8[:, c, t * P:(t + 1) * P], lambda c: w[:, c, 0:256], 256)
            for m in range(2):
                rows_times(lambda c: w[:, c, 256 + m * P:256 + (m + 1) * P],
                           lambda c: hT8[:, c, 0:nt * P], nt * P)
            release(g)
            g += 1
            w = tile(g)
            for m in (0, 2, 1, 3):
                rows_times(lambda c: w[:, c, m * P:(m + 1) * P], lambda c: hT8[:, c, 0:nt * P], nt * P)
            release(g)
            g += 1
            for t in range(4):
                need("qk", qk_ready)
                if t < nt:
                    turn([hb[:, t, i * P:(i + 1) * P] for i in range(4)])
                turn([hb[:, t, 512 + i * P:512 + (i + 1) * P] for i in range(2)])
            pe.wait_ge(tp_free, T["tp"])
            need("v", v_ready)
            for t in range(nt):
                bank = acc_bank()
                for q in range(4):
                    last = mm(bank[:, q * 64:(q + 1) * 64], gmw[:, q, :],
                              guv[:, t, 256 + q * 64:256 + (q + 1) * 64], start=True, stop=True)
                last.then_inc(acc_full, 1)
            attention([(n, h) for n in range(NX) for h in range(NH)],
                      gqa_score(qTA, kTA, lambda n: 0, lambda n: 512),
                      lambda n, h, k: vA[:, k, (h // GQA) * HD:(h // GQA + 1) * HD], 4, HD)
            if nt == 4:
                attention([(n, h) for n in range(NX, 4) for h in range(NH)],
                          gqa_score(qTA, kTA, lambda n: 256, lambda n: 512),
                          lambda n, h, k: vA[:, 2 + k, (h // GQA) * HD:(h // GQA + 1) * HD], 2, HD)
            for t in range(nt):
                need("h", h_ready)
                turn([hb[:, t, i * P:(i + 1) * P] for i in range(4)])
                turn([hb[:, t, (6 + i) * P:(7 + i) * P] for i in range(2)])
            pe.wait_ge(tp_free, T["tp"])
            need("v", v_ready)
            for j in range(OUT_TILES):
                w = tile(g)
                for t in range(nt):
                    rows_times(lambda c: hT8[:, c, t * P:(t + 1) * P], lambda c: w[:, c, :], 512)
                release(g)
                g += 1

            for t in range(nt):
                need("h", h_ready)
                turn_rows(t, hb[:, t, :], DC)
            pe.wait_ge(tp_free, T["tp"])
            pe.wait_ge(par_in, par_a(l, 10))
            for t in range(nt):
                rows_times(lambda c: hT8[:, c, t * P:(t + 1) * P], lambda c: wr[:, c, :], 36)
            need("v", v_ready)
            bank = acc_bank()
            for t in range(nt):
                for u in range(t):
                    mm(bank[:, t * E:(t + 1) * E], const("ones"), mem_[:, u, :], start=(u == 0), stop=False)
                mm(bank[:, t * E:(t + 1) * E], const("ustrict"), mem_[:, t, :], start=(t == 0), stop=True)
            for u in range(nt):
                last = mm(bank[:, 4 * E:5 * E], const("ones"), mem_[:, u, :], start=(u == 0), stop=(u == nt - 1))
            last.then_inc(acc_full, 1)
            need("v", v_ready)
            bank = acc_bank()
            nb = E + OVERFLOW[l]
            for k in range(2):
                for t in range(nt):
                    last = mm(bank[:, 0:nb], R[k][:, t, :], bo[k][:, t, 0:nb],
                              start=(k == 0 and t == 0), stop=(k == 1 and t == nt - 1))
            last.then_inc(acc_full, 1)
            B0, X0, G0 = blocks_before[l], gathers_before[l], baseM[l]
            pe.wait_ge(acc_free, T["acc"])
            pe.wait_ge(tp_free, T["tp"])
            pe.wait_ge(sc_free, T["sc"])

            def turn_tokens(u, landed):
                pe.wait_ge(m_xg[u], landed)
                for j in range(2):
                    for i in range(4):
                        c = 4 * j + i
                        last = nc.tensor.transpose(ps[:, 4 + j, i * P:(i + 1) * P],
                                                   xg[:, u, c * P:(c + 1) * P], ident)
                    last.then_inc(m_xt, 1)

            def products(bank, w, n, cols, lhs, is_wide):
                half = cols // 2
                for c in range(n):
                    for q in range(2 if not is_wide or cols > 512 else 1):
                        if not is_wide:
                            out = ps[64 * q:64 * q + 64, bank + (q if cols > 512 else 0),
                                     0 if cols > 512 else half * q:half if cols > 512 else half * (q + 1)]
                            last = mm(out, lhs(c)[:, 0:64], w(c)[:, half * q:half * (q + 1)],
                                      start=(c == 0), stop=(c == n - 1))
                        elif cols > 512:
                            last = mm(ps[:, bank + q, :], lhs(c), w(c)[:, half * q:half * (q + 1)],
                                      start=(c == 0), stop=(c == n - 1))
                        else:
                            last = mm(ps[:, bank, :], lhs(c), w(c), start=(c == 0), stop=(c == n - 1))
                return last

            pe.wait_ge(idx_ready, l + 1)
            turn_tokens(0, 16 * (gpar_before[l][0] + 1))
            with pe.Fori(0, E // UNROLL) as i:
                for u in range(UNROLL):
                    p = u % 2

                    def moe_tile(k):
                        q = G0 + 3 * u + k
                        pe.wait_ge(ring_full[q % RING], i * 48 + 16 * (q // RING + 1))
                        return ring[:, q % RING, :, :]

                    b = i * UNROLL + (B0 + u)
                    pe.wait_ge(m_xe, i * (2 * UNROLL) + 2 * (X0 + u + 1))
                    w = (moe_tile(0), moe_tile(1))
                    is_wide = pe.value_load(wide[0:1, bass.ds(i * UNROLL + u, 1)], min_val=0, max_val=1)

                    def up(flag):
                        for k, (bank, done) in enumerate(((p, m_h1), (2 + p, m_h3))):
                            products(bank, lambda c: w[k][:, c, :], DC, 512, lambda c: xgT[:, p, c, :],
                                     flag).then_inc(done, 1)

                    with pe.If(is_wide > 0):
                        up(True)
                    with pe.Else():
                        up(False)
                    turn_tokens(1 - p, i * 32 + 16 * (gpar_before[l][1 - p] + (u + 1) // 2 + 1))
                    pe.wait_ge(m_g, b + 1)
                    w2_ = moe_tile(2).rearrange("p (k n) x -> p k (n x)", n=2)

                    def down(flag):
                        for c in range(4):
                            bank, o = p + 2 * (c // 2), (c % 2) * P
                            if flag:
                                last = nc.tensor.transpose(ps[:, bank, o:o + P],
                                                           gbuf[:, p, c * P:(c + 1) * P], ident)
                            else:
                                r = slice(64 * (c // 2), 64 * (c // 2) + 64)
                                last = nc.tensor.transpose(ps[:, bank, o:o + 64],
                                                           gbuf[r, p, c * P:(c + 1) * P], ident[r, r])
                        last.then_inc(m_gt, 1)
                        pe.wait_ge(m_ge, b + 1)
                        products(6, lambda c: w2_[:, c, :], 4, D, lambda c: gT[:, p, c, :],
                                 flag).then_inc(m_y, 1)

                    with pe.If(is_wide > 0):
                        down(True)
                    with pe.Else():
                        down(False)
            pe.wait_ge(m_xe, 2 * (X0 + E + 1))
            pe.wait_ge(m_ye, B0 + E)
            o = ov[l]
            slots = [(G0 + 3 * E + k) % RING for k in range(3)]
            pe.wait_ge(idx_ready, l + 1)
            n_over = pe.value_load(ovid[0:1, 8:9], min_val=0, max_val=8)
            with pe.If(n_over > 0):
                with pe.Fori(0, OVERFLOW[l]) as j:
                    pe.wait_ge(o["rows_in"], j * 16 + 16)
                    for c in range(DC):
                        last = nc.tensor.transpose(ps[:, 4 + c // 4, (c % 4) * P:(c % 4 + 1) * P],
                                                   xg[:, 0, c * P:(c + 1) * P], ident)
                    last.then_inc(o["turned"], 1)
                    pe.wait_ge(o["rows_T"], j + 1)
                    pe.wait_ge(o["w1_in"], j * 16 + 16)
                    for c in range(DC):
                        mm(ps[:, 0, :], xgT[:, 0, c, :], ring[:, slots[0], c, :], start=(c == 0), stop=(c == DC - 1))
                    pe.wait_ge(o["w3_in"], j * 16 + 16)
                    for c in range(DC):
                        last = mm(ps[:, 2, :], xgT[:, 0, c, :], ring[:, slots[1], c, :], start=(c == 0),
                                  stop=(c == DC - 1))
                    last.then_inc(o["h13"], 1)
                    pe.wait_ge(o["gated"], j + 1)
                    for c in range(4):
                        last = nc.tensor.transpose(ps[:, 0, c * P:(c + 1) * P], gbuf[:, 0, c * P:(c + 1) * P], ident)
                    last.then_inc(o["gated_turned"], 1)
                    pe.wait_ge(o["gated_T"], j + 1)
                    pe.wait_ge(o["w2_in"], j * 16 + 16)
                    w = ring[:, slots[2], :, :].rearrange("p (k n) x -> p k (n x)", n=2)
                    for n in range(2):
                        for c in range(4):
                            last = mm(ps[:, 6 + n, :], gT[:, 0, c, :], w[:, c, n * 512:(n + 1) * 512],
                                      start=(c == 0), stop=(c == 3))
                    last.then_inc(o["y"], 1)

        for l in range(DEPTH):
            g = baseB[l]
            for t in range(NX):
                need("h", h_ready)
                for c in (0, 4):
                    turn([hB[:, t, (c + i) * P:(c + i + 1) * P] for i in range(4)])
            pe.wait_ge(tp_free, T["tp"])

            def rows(cols, off=0):
                nonlocal g
                w = tile(g)
                for t in range(NX):
                    rows_times(lambda c: hT16[:, off + c, t * P:(t + 1) * P], lambda c: w[:, c, 0:cols], cols)
                release(g)
                g += 1

            def cols_T(off=0):
                nonlocal g
                w = tile(g)
                for m in range(0, 4, 2):
                    bank = acc_bank()
                    for q in range(2):
                        for c in range(DC):
                            last = mm(bank[:, q * 256:(q + 1) * 256], w[:, c, (m + q) * P:(m + q + 1) * P],
                                      hT16[:, off + c, :], start=(c == 0), stop=(c == DC - 1))
                    last.then_inc(acc_full, 1)
                release(g)
                g += 1

            rows(512)
            rows(280)
            rows(512)
            cols_T()
            cols_T()
            rows(512)
            rows(512)
            rows(512)
            rows(512)
            for _ in range(3):
                cols_T()
            for t in range(NX):
                need("qk", qk_ready)
                turn([mixB[:, t, i * P:(i + 1) * P] for i in range(4)])
                turn([mixB[:, t, 512 + i * P:512 + (i + 1) * P] for i in range(2)])
            pe.wait_ge(tp_free, T["tp"])
            attention([(n, h) for n in range(NX) for h in range(NH)],
                      gqa_score(qaT, kaT, lambda n: 0, lambda n: 256),
                      lambda n, h, k: vaB[:, k, (h // GQA) * HD:(h // GQA + 1) * HD], 2, HD)
            need("v", v_ready)
            bank = acc_bank()
            spf = sp[3]
            for t in range(NX):
                mm(bank[:, 16 * t:16 * t + 16], const("uincl"), dta[:, t, :], start=True, stop=True)
                mm(bank[:, 32 + 16 * t:48 + 16 * t], const("ones"), dta[:, t, :], start=True, stop=True)
            mm(bank[:, 64:72], const("uincl"), spf[:, 0, 0:8], start=True, stop=True)
            mm(bank[:, 72:80], const("ones"), spf[:, 0, 0:8], start=True, stop=False)
            mm(bank[:, 72:80], const("uincl"), spf[:, 1, 0:8], start=False, stop=True).then_inc(acc_full, 1)

            def fox_score(n, h):
                bank = sc_bank()
                o = HD * (h % 2)
                mm(bank[:, 0:256], qbT[o:o + HD, h // 2, n * P:(n + 1) * P], kbT[o:o + HD, h // 2, :],
                   start=True, stop=False)
                mm(bank[:, 0:256], spf[:, 0, h:h + 1].to_broadcast([P, P]), const("uincl", 256),
                   start=False, stop=False)
                mm(bank[:, 0:256], spf[:, 1, h:h + 1].to_broadcast([P, P]), const("z0", 256),
                   start=False, stop=True).then_inc(sc_full, 1)

            attention([(n, h) for n in range(NX) for h in range(NH)], fox_score,
                      lambda n, h, k: vbB[:, k, h * HD:(h + 1) * HD], 2, HD)
            for t in range(NX):
                for c in (0, 4):
                    turn([xc[:, c + i, t * P:(t + 1) * P] for i in range(4)])
            turn([xc[:, 8 + i, 0:P] for i in range(2)])
            for t in range(NX):
                bank = acc_bank()
                for q in range(2):
                    last = mm(bank[:, q * P:(q + 1) * P], xc[:, 8 + q, t * P:(t + 1) * P],
                              xc[:, 10 + q, t * P:(t + 1) * P], start=True, stop=True)
                last.then_inc(acc_full, 1)
            need("v", v_ready)
            pe.wait_ge(tp_free, T["tp"])
            for q in range(2):
                bank = acc_bank()
                mm(bank, bmn[:, q * P:(q + 1) * P], xds[:, q * 512:(q + 1) * 512],
                   start=True, stop=True).then_inc(acc_full, 1)

            def decay(i):
                t, q4 = i // 4, i % 4
                bank = sc_bank()
                for q in range(4):
                    h = 4 * q4 + q
                    last = mm(bank[:, q * P:(q + 1) * P], dta[:, t, h:h + 1].to_broadcast([P, P]),
                              const("uincl"), start=True, stop=True)
                last.then_inc(sc_full, 1)

            decay(0)
            decay(1)
            for i in range(8):
                t, q4 = i // 4, i % 4
                need("w", w_ready)
                if i + 2 < 8:
                    decay(i + 2)
                if q4 % 2 == 0:
                    bank = acc_bank()
                for q in range(4):
                    h = 4 * q4 + q
                    o = (h % 8) * HD
                    last = mm(bank[:, o:o + HD], W2[:, i % 2, q * P:(q + 1) * P],
                              xdt[:, t, h * HD:(h + 1) * HD], start=True, stop=True)
                if q4 % 2 == 1:
                    last.then_inc(acc_full, 1)
                    if t == 1:
                        bank = acc_bank()
                        need("v", v_ready) if q4 == 1 else None
                        mm(bank, xc[:, 10 + q4 // 2, P:2 * P], stT[:, q4 // 2, :],
                           start=True, stop=True).then_inc(acc_full, 1)
            for t in range(NX):
                need("h", h_ready)
                for c in range(0, 16, 4):
                    turn([mixB[:, t, (c + i) * P:(c + i + 1) * P] for i in range(4)])
            pe.wait_ge(tp_free, T["tp"])
            for n in range(2):
                wa, wb = tile(g), tile(g + 1)
                for t in range(NX):
                    rows_times(lambda c: hT16[:, c, t * P:(t + 1) * P],
                               lambda c: (wa if c < 8 else wb)[:, c % 8, :], 512, n=16)
                release(g)
                release(g + 1)
                g += 2
            for t in range(NX):
                need("h", h_ready)
                for c in (0, 4):
                    turn([memn[:, t, (c + i) * P:(c + i + 1) * P] for i in range(4)])
            for t in range(NX):
                need("h", h_ready)
                for c in (0, 4):
                    turn([hB[:, t, (c + i) * P:(c + i + 1) * P] for i in range(4)])
            pe.wait_ge(tp_free, T["tp"])
            cols_T(8)
            cols_T(8)
            rows(512, 8)
            rows(512, 8)
            cols_T()
            cols_T()

            def mem_score(n, h):
                bank = sc_bank()
                for k in range(2):
                    last = mm(bank[:, 0:256], qmT[:, 2 * h + k, n * P:(n + 1) * P], kmT[:, 2 * h + k, :],
                              start=(k == 0), stop=(k == 1))
                last.then_inc(sc_full, 1)

            need("v", v_ready)
            attention([(n, h) for n in range(NX) for h in range(4)], mem_score,
                      lambda n, h, k: vm[:, k, h * 256:(h + 1) * 256], 2, 256)
            for t in range(NX):
                need("h", h_ready)
                for c in (0, 4):
                    turn([mixB[:, t, (c + i) * P:(c + i + 1) * P] for i in range(4)])
            pe.wait_ge(tp_free, T["tp"])
            rows(512)
            rows(512)

    @block.sync
    def _(sp_):
        sp_.dma_start(cst[:, :], d["consts"]).then_inc(const_in, 16)
        sp_.dma_start(S[:, 0:2, :], d["x"].rearrange("(t p) n -> p t n", p=P)).then_inc(const_in, 16)
        sp_.dma_start(S[:, 2:4, :], d["ctx"].rearrange("(t p) n -> p t n", p=P)).then_inc(const_in, 16)

        def slot(g):
            if g >= RING:
                s, v = released[g - RING]
                sp_.wait_ge(s, v)
            return ring[:, g % RING, :, :].rearrange("p c n -> p (c n)")

        def dense(src, n, g):
            for i in range(n):
                dst = slot(g + i)
                sp_.dma_start(dst, src[i]).then_inc(ring_full[(g + i) % RING], 16)

        for l in range(DEPTH):
            dense(d["denseA"][l], SEG_A, baseA[l])
            G0, B0 = baseM[l], blocks_before[l]
            dense(d["moe"][l], 3 * UNROLL, G0)
            with sp_.Fori(0, E // UNROLL - 1) as i:
                for j in range(3 * UNROLL):
                    q = j - RING
                    s = (m_h1, m_h3, m_y)[q % 3]
                    sp_.wait_ge(s, i * UNROLL + (B0 + UNROLL + q // 3 + 1))
                    sp_.dma_start(ring[:, (G0 + j) % RING, :, :].rearrange("p c n -> p (c n)"),
                                  d["moe"][l][i * (3 * UNROLL) + (3 * UNROLL + j)]).then_inc(ring_full[(G0 + j) % RING], 16)
            o = ov[l]
            sp_.wait_ge(idx_ready, l + 1)
            n_over = sp_.value_load(ovid[0:1, 8:9], min_val=0, max_val=8)
            with sp_.If(n_over > 0):
                sp_.wait_ge(m_y, B0 + E)
                for j in range(OVERFLOW[l]):
                    if j > 0:
                        sp_.wait_ge(o["y"], j)
                    e = sp_.value_load(ovid[0:1, j:j + 1], min_val=0, max_val=E - 1)
                    for k, n in enumerate(("w1_in", "w3_in", "w2_in")):
                        sp_.dma_start(ring[:, (G0 + 3 * E + k) % RING, :, :].rearrange("p c n -> p (c n)"),
                                      d["moe"][l][e * 3 + k]).then_inc(o[n], 16)
                sp_.wait_ge(o["y"], OVERFLOW[l])
        for l in range(DEPTH):
            dense(d["denseB"][l], SEG_B, baseB[l])
        sp_.wait_ge(out_ready, 1)
        sp_.dma_start(d["out"].rearrange("(t p) n -> p t n", p=P), hb[:, 0:2, :]).then_inc(out_done, 16)
        sp_.wait_ge(out_done, 16)

    @block.gpsimd
    def _(pool):
        T = defaultdict(int)

        def load(dst, src, s):
            pool.dma_start(dst, src).then_inc(s, 16)

        def used(n=1):
            T["used"] += n
            pool.wait_ge(mod_used, T["used"])

        for p in range(2):
            load(idcol[0:1, p:p + 1], d["consts"].bitcast(I32)[0:1, 0:1], m_yw[p])
        for l in range(DEPTH):
            nt = 4 if l < DEPTH - 1 else NX
            if l > 0:
                pool.wait_ge(phase, 2 * (2 * l))
            bada = d["b_ada"][l:l + 1, :].rearrange("a (n j x) -> a j n x", n=ADA_TILES, j=4)
            for j in range(4):
                load(mst[32 * j:32 * j + 32, :, :], bada[:, j, :, :].to_broadcast([32, ADA_TILES, P]), bada_in)
            if l == 0:
                load(cact[:, :, :].rearrange("p a b -> p (a b)"), d["cpack"], bada_in)
            load(snk, d["attn_sink"][l:l + 1, :].to_broadcast([P, NH]), par_in)
            load(gmb, d["gm_bs"][l], par_in)
            load(cwA.rearrange("p a b -> p (a b)"), d["conv_w"][l], par_in)
            load(lnB[:, 0, :], d["ln1_g"][l:l + 1, :].to_broadcast([P, D]), par_in)
            load(lnB[:, 1, :], d["ln1_b"][l:l + 1, :].to_broadcast([P, D]), par_in)
            for half in range(2):
                T["rr"] += 1
                pool.wait_ge(rows_ready, T["rr"])
                sl = slice(half * ADA_TILES // 2, (half + 1) * ADA_TILES // 2)
                for r in range(2):
                    load(mod_d[l, r].rearrange("(n j x) -> j n x", n=ADA_TILES, j=4)[:, sl, :],
                         mst[r:P:32, sl, :], rows_out)
                T["ro"] += 32
                pool.wait_ge(rows_out, T["ro"])
                if half == 0:
                    for r in range(2):
                        for k in range(2):
                            load(modB[:, 2 * r + k, :],
                                 mod_d[l, r:r + 1, k * D:(k + 1) * D].to_broadcast([P, D]), mod_in)
            load(gmw.rearrange("p a b -> p (a b)"), d["gm_ws"][l], par_in)
            used()
            for r in range(2 if nt == 4 else 1):
                load(modB[:, r, :], mod_d[l, r:r + 1, 2 * D:3 * D].to_broadcast([P, D]), mod_in)
            used()
            for r in range(2 if nt == 4 else 1):
                for k in range(2):
                    load(modB[:, 2 * r + k, :],
                         mod_d[l, r:r + 1, (3 + k) * D:(4 + k) * D].to_broadcast([P, D]), mod_in)
            load(lnB[:, 0, :], d["ln2_g"][l:l + 1, :].to_broadcast([P, D]), par_in)
            load(lnB[:, 1, :], d["ln2_b"][l:l + 1, :].to_broadcast([P, D]), par_in)
            pool.wait_ge(phase, 2 * (2 * l + 1))
            load(wr.rearrange("p a b -> p (a b)"), d["w_route"][l], par_in)
            load(rb, d["b_route"][l:l + 1, :].to_broadcast([P, 36]), par_in)
            for t in range(nt):
                T["h2"] += 1
                pool.wait_ge(tok_ready, T["h2"])
                pool.dma_start(tok_d[t * P:(t + 1) * P, :], hb[:, t, :]).then_inc(tok_out, 16)
                T["to"] += 16
            used()
            for r in range(2 if nt == 4 else 1):
                load(modB[:, r, :], mod_d[l, r:r + 1, 5 * D:6 * D].to_broadcast([P, D]), mod_in)
            pool.wait_ge(tok_out, T["to"])
            pool.wait_ge(idx_ready, l + 1)
            B0, X0 = blocks_before[l], gathers_before[l]
            nc.gpsimd.tensor_copy(idcol[:, 0:1], slot_tok[:, 0:1]).then_inc(pool_step, 1)
            pool.wait_ge(pool_step, X0 + 1)
            pool.indirect_dma_start(xg[:, 0, :], None, tok_d,
                                    bass.IndirectOffsetOnAxis(ap=idcol[:, 0:1], axis=0)).then_inc(m_xg[0], 16)
            with pool.Fori(0, E // UNROLL) as i:
                for u in range(UNROLL):
                    p = (u + 1) % 2
                    pool.wait_ge(m_xt, i * (2 * UNROLL) + 2 * (X0 + u + 1))
                    nc.gpsimd.tensor_copy(idcol[:, p:p + 1],
                                          slot_tok[:, bass.ds(i * UNROLL + (u + 1), 1)]).then_inc(pool_step, 1)
                    pool.wait_ge(pool_step, i * UNROLL + (X0 + u + 2))
                    pool.nop(nofuse=True)
                    pool.indirect_dma_start(xg[:, p, :], None, tok_d,
                                            bass.IndirectOffsetOnAxis(ap=idcol[:, p:p + 1], axis=0)
                                            ).then_inc(m_xg[p], 16)
                    pool.wait_ge(m_ye, i * UNROLL + (B0 + u + 1))
                    pool.dma_start(ys_d[bass.ds(i * (UNROLL * P) + u * P, P), :],
                                   ysb[:, u % 2, :]).then_inc(m_yw[u % 2], 16)
            for p in range(2):
                pool.wait_ge(m_yw[p], 16 * ((B0 + E) // 2 + 1))
            pool.wait_ge(m_xg[0], 16 * (gpar_before[l][0] + E // 2 + 1))
            pool.wait_ge(m_xg[1], 16 * (gpar_before[l][1] + E // 2))
            pool.wait_ge(m_xt, 2 * (X0 + E + 1))
            pool.wait_ge(ys_init, 16)
            o = ov[l]
            n_over = pool.value_load(ovid[0:1, 8:9], min_val=0, max_val=8)
            with pool.If(n_over > 0):
                with pool.Fori(0, OVERFLOW[l]) as j:
                    nc.gpsimd.tensor_copy(idcol[:, 0:1], slot_tok[:, bass.ds(j + E, 1)]).then_inc(o["ids"], 1)
                    pool.wait_ge(o["ids"], j + 1)
                    pool.nop(nofuse=True)
                    pool.indirect_dma_start(xg[:, 0, :], None, tok_d,
                                            bass.IndirectOffsetOnAxis(ap=idcol[:, 0:1], axis=0)
                                            ).then_inc(o["rows_in"], 16)
                    pool.wait_ge(o["y_copied"], j + 1)
                    pool.dma_start(ys_d[bass.ds(j * P + E * P, P), :], ysb[:, 0, :]).then_inc(o["y_out"], 16)
                    pool.wait_ge(o["y_out"], j * 16 + 16)
            for t in range(nt):
                if t >= 2:
                    T["cu"] += 1
                    pool.wait_ge(comb_used, T["cu"])
                for k in range(2):
                    for h in range(2):
                        pool.indirect_dma_start(yg[k][:, t % 2, h * 512:(h + 1) * 512], None,
                                                ys_d.rearrange("r (h n) -> (r h) n", h=2),
                                                bass.IndirectOffsetOnAxis(ap=dest[:, t, k, h:h + 1], axis=0)
                                                ).then_inc(comb_in[t % 2], 16)
        for l in range(DEPTH):
            pool.wait_ge(phase, 2 * (4 + 2 * l))
            load(lnB[:, 0, :], d["norm_mix_w_2"][l:l + 1, :].to_broadcast([P, D]), par_in)
            load(lnB[:, 1, :], d["ssm_norm_w_2"][l:l + 1, :].to_broadcast([P, D]), par_in)
            load(snk, d["swa_sinks_2"][l:l + 1, :].to_broadcast([P, NH]), par_in)
            load(bfd[:, 0:8], d["b_forget_2"][l:l + 1, :].to_broadcast([P, 8]), par_in)
            load(bfd[:, 8:24], d["dt_bias_2"][l:l + 1, :].to_broadcast([P, 16]), par_in)
            load(aneg, d["a_log_2"][l:l + 1, :].to_broadcast([P, 16]), par_in)
            load(dskip, d["d_skip_2"][l:l + 1, :].to_broadcast([P, 16]), par_in)
            load(cwB.rearrange("p a b -> p (a b)"), d["conv_w_2"][l], par_in)
            load(cbB, d["conv_b_2"][l], par_in)
            pool.wait_ge(phase, 2 * (4 + 2 * l + 1))
            load(memn[:, :, :], d["mem_2"].rearrange("(t p) n -> p t n", p=P), par_in)
            load(lnB[:, 0, :], d["norm_xq_w_2"][l:l + 1, :].to_broadcast([P, D]), par_in)
            load(lnB[:, 1, :], d["norm_mem_w_2"][l:l + 1, :].to_broadcast([P, D]), par_in)
        pool.wait_ge(phase, 2 * 8)
        load(lnB[:, 0, :], d["final_norm_w_2"].rearrange("(a n) -> a n", a=1).to_broadcast([P, D]), par_in)

    @block.scalar
    def _(act):
        T = defaultdict(int)
        A = nc.scalar.activation

        def copy_turned(out, n, scale=None):
            T["tp"] += 1
            act.wait_ge(tp_full, T["tp"])
            src = tpb(T["tp"] - 1)[:, 0:n * P].rearrange("p (c x) -> p c x", c=n)
            A(out, src, ACT.Copy, scale=1.0 if scale is None else scale).then_inc(tp_free, 1)

        def for_dve(f):
            T["d2a"] += 1
            act.wait_ge(dve_to_act, T["d2a"])
            f().then_inc(act_to_dve, 1)

        def attention(units, nk, nkc, sink, heads):
            for i, (n, h) in enumerate(units):
                T["nm"] += 1
                act.wait_ge(nm_ready, T["nm"])
                A(sbuf_p[:, i % 2, 0:nk], sbuf_s[:, i % 2, 0:nk], ACT.Exp, bias=nm[:, n, h:h + 1],
                  accum_out=rsum[:, n, h:h + 1]).then_inc(p_ready, 1)
                copy_turned(sbuf_pT[:, i % 2, 0:nkc, :], nkc)
                if sink and h == heads - 1:
                    for_dve(lambda: A(esk, esk, ACT.Exp))

        def leave():
            for_dve(lambda: A(mx[:, 1:2], mx[:, 1:2], ACT.Copy))
            act.wait_ge(act_to_dve, T["d2a"])
            act.sem_inc(phase, 1)

        for l in range(DEPTH):
            nt = 4 if l < DEPTH - 1 else NX
            if l == 0:
                act.wait_ge(const_in, 48)
                act.dma_start(ys_d[E * P:, :].rearrange("(b p) n -> p b n", p=P),
                              cst[:, 0:D].unsqueeze(1).to_broadcast([P, OVERFLOW[0], D])).then_inc(ys_init, 16)
                act.wait_ge(bada_in, 80)
                A(ce, cact[:, :, :], ACT.Exp, scale=-1.0).then_inc(c_exp, 1)
            for t in range(4):
                for c in (0, 4):
                    copy_turned(hT8[:, c:c + 4, t * P:(t + 1) * P], 4)
            for t in range(4):
                if t < nt:
                    copy_turned(qTA[:, :, t * P:(t + 1) * P], 4, QSCALE)
                copy_turned(kTA[:, :, t * P:(t + 1) * P], 2)
            for_dve(lambda: A(guv[:, 0:nt, :], guv[:, 0:nt, :], ACT.Gelu_apprx_tanh))
            for_dve(lambda: A(rstd[:, 0:nt], rstd[:, 0:nt], ACT.Sqrt))
            attention([(n, h) for n in range(NX) for h in range(NH)], 512, 4, True, NH)
            if nt == 4:
                attention([(n, h) for n in range(NX, 4) for h in range(NH)], 256, 2, True, NH)
            for t in range(nt):
                copy_turned(hT8[:, 0:4, t * P:(t + 1) * P], 4)
                copy_turned(hT8[:, 6:8, t * P:(t + 1) * P], 2)
            for_dve(lambda: A(rstd[:, 0:nt], rstd[:, 0:nt], ACT.Sqrt))
            leave()
            for t in range(nt):
                for c in (0, 4):
                    copy_turned(hT8[:, c:c + 4, t * P:(t + 1) * P], 4)
            for_dve(lambda: A(g4[0][:, 0:nt, :], g4[0][:, 0:nt, :], ACT.Exp))
            for_dve(lambda: A(rt[2][:, 0:nt], rt[2][:, 0:nt], ACT.Exp))
            B0, X0 = blocks_before[l], gathers_before[l]

            def token_copies(p, job):
                for j in range(2):
                    act.wait_ge(m_xt, job + j)
                    A(xgT[:, p, 4 * j:4 * j + 4, :], ps[:, 4 + j, :].rearrange("p (c x) -> p c x", c=4),
                      ACT.Copy).then_inc(m_xe, 1)

            act.wait_ge(idx_ready, l + 1)
            token_copies(0, 2 * X0 + 1)
            with act.Fori(0, E // UNROLL) as i:
                for u in range(UNROLL):
                    p = u % 2
                    b = i * UNROLL + (B0 + u)
                    act.wait_ge(m_h1, b + 1)
                    A(eb[:, p, :], ps[:, p, :], ACT.Silu).then_inc(m_e, 1)
                    token_copies(1 - p, i * (2 * UNROLL) + (2 * (X0 + u + 1) + 1))
                    act.wait_ge(m_gt, b + 1)
                    A(gT[:, p, :, :].rearrange("p (b c) x -> p b (c x)", b=2), ps[:, p:p + 3:2, 0:256],
                      ACT.Copy).then_inc(m_ge, 1)
            o = ov[l]
            n_over = act.value_load(ovid[0:1, 8:9], min_val=0, max_val=8)
            with act.If(n_over > 0):
                with act.Fori(0, OVERFLOW[l]) as j:
                    act.wait_ge(o["turned"], j + 1)
                    for q in range(2):
                        last = A(xgT[:, 0, 4 * q:4 * q + 4, :], ps[:, 4 + q, :].rearrange("p (c x) -> p c x", c=4),
                                 ACT.Copy)
                    last.then_inc(o["rows_T"], 1)
                    act.wait_ge(o["h13"], j + 1)
                    A(eb[:, 0, :], ps[:, 0, :], ACT.Silu).then_inc(o["silu"], 1)
                    act.wait_ge(o["gated_turned"], j + 1)
                    A(gT[:, 0, :, :], ps[:, 0, :].rearrange("p (c x) -> p c x", c=4),
                      ACT.Copy).then_inc(o["gated_T"], 1)
            for_dve(lambda: A(rstd[:, 0:nt], rstd[:, 0:nt], ACT.Sqrt))
            leave()

        def silu(buf):
            for_dve(lambda: A(buf, buf, ACT.Silu))

        for l in range(DEPTH):
            for_dve(lambda: A(rstd[:, 0:NX], rstd[:, 0:NX], ACT.Sqrt))
            for t in range(NX):
                for c in (0, 4):
                    copy_turned(hT16[:, c:c + 4, t * P:(t + 1) * P], 4)
            for t in range(NX):
                copy_turned(qaT[:, :, t * P:(t + 1) * P], 4, QSCALE)
                copy_turned(kaT[:, :, t * P:(t + 1) * P], 2)
            silu(modB[:, :, :])
            silu(xc[:, :, :])
            for_dve(lambda: A(sp[1][:, :, :], sp[1][:, :, :], ACT.Exp, scale=-1.0))
            for_dve(lambda: A(aneg, aneg, ACT.Exp))
            attention([(n, h) for n in range(NX) for h in range(NH)], 256, 2, True, NH)
            attention([(n, h) for n in range(NX) for h in range(NH)], 256, 2, False, NH)
            for t in range(NX):
                for c in (0, 4):
                    copy_turned(xsn[:, t, c * P:(c + 4) * P].rearrange("p (c x) -> p c x", c=4), 4)
            copy_turned(bmn.rearrange("p (c x) -> p c x", c=2), 2)
            for_dve(lambda: A(dst, dst, ACT.Exp))
            for_dve(lambda: A(eacs, cs[:, 16:32], ACT.Exp))
            for i in range(8):
                for_dve(lambda: A(W[:, i % 2, :], W[:, i % 2, :], ACT.Exp))
            for_dve(lambda: A(rstd[:, 0:NX], rstd[:, 0:NX], ACT.Sqrt))
            for t in range(NX):
                for c in range(0, 16, 4):
                    copy_turned(hT16[:, c:c + 4, t * P:(t + 1) * P], 4)
            leave()
            for_dve(lambda: A(rstd[:, 0:NX], rstd[:, 0:NX], ACT.Sqrt))
            for t in range(NX):
                for c in (0, 4):
                    copy_turned(hT16[:, 8 + c:12 + c, t * P:(t + 1) * P], 4)
            for_dve(lambda: A(rstd[:, 0:NX], rstd[:, 0:NX], ACT.Sqrt))
            for t in range(NX):
                for c in (0, 4):
                    copy_turned(hT16[:, c:c + 4, t * P:(t + 1) * P], 4)
            attention([(n, h) for n in range(NX) for h in range(4)], 256, 2, False, 4)
            for t in range(NX):
                for c in (0, 4):
                    copy_turned(hT16[:, c:c + 4, t * P:(t + 1) * P], 4)
            leave()
        for_dve(lambda: A(rstd[:, 0:NX], rstd[:, 0:NX], ACT.Sqrt))

    @block.vector
    def _(dve):
        T = defaultdict(int)
        V = nc.vector

        def step(ins):
            T["dve"] += 1
            ins.then_inc(dve_step, 1)
            dve.wait_ge(dve_step, T["dve"])

        def go(ins):
            T["dve"] += 1
            ins.then_inc(dve_step, 1)

        def done():
            dve.wait_ge(dve_step, T["dve"])

        def tell(ins, s):
            T[s.name] += 1
            ins.then_inc(s, 1)
            dve.wait_ge(s, T[s.name])

        def tt(out, a, b, op):
            return V.tensor_tensor(out, a, b, op)

        def ts(out, a, s1, s2, op0, op1=None):
            if op1 is None:
                return V.tensor_scalar(out, a, s1, None, op0)
            return V.tensor_scalar(out, a, s1, s2, op0, op1)

        def stt(out, a, s, b, op0, op1):
            return V.scalar_tensor_tensor(out=out, in0=a, scalar=s, in1=b, op0=op0, op1=op1)

        def acc_job():
            T["acc"] += 1
            dve.wait_ge(acc_full, T["acc"])
            return acc(T["acc"] - 1)

        def read(ins):
            tell(ins, acc_free)

        def by_act(ins=None):
            if ins is None:
                ins = V.tensor_copy(mx[:, 1:2], mx[:, 0:1])
            ins.then_inc(dve_to_act, 1)
            T["a2d"] += 1
            dve.wait_ge(act_to_dve, T["a2d"])

        def rope(out, bank, heads, table, t, halves):
            w = HD // halves // 2
            c = const(table, HD, t * 128).unsqueeze(1).to_broadcast([P, heads, HD])
            step(tt(out, bank.rearrange("p (h x) -> p h x", h=heads), c, ALU.mult))
            s = const(table, HD, t * 128 + 64).rearrange("p (f b w) -> p f b w", f=halves, b=2)
            tmp = ropet[:, 0:heads * HD].rearrange("p (h f b w) -> p h f b w", h=heads, f=halves, b=2)
            x = bank.rearrange("p (h f b w) -> p h f b w", h=heads, f=halves, b=2)
            for f in range(halves):
                for b in range(2):
                    sl = s[:, f, b, :].unsqueeze(1).to_broadcast([P, heads, w])
                    ins = tt(tmp[:, :, f, b, :], x[:, :, f, 1 - b, :], sl, ALU.mult)
                    if f == halves - 1 and b == 1:
                        read(ins)
                    else:
                        step(ins)
            return tt(out, out, ropet[:, 0:heads * HD].rearrange("p (h x) -> p h x", h=heads), ALU.add)

        def attention(units, nk, masks, cq, sink, heads, hw, finish):
            per = 512 // hw
            rest = []

            def close(n, hq):
                if hq == 0:
                    if sink:
                        step(tt(esk, snk, nm[:, n, 0:heads], ALU.add))
                        by_act()
                        step(tt(rsum[:, n, 0:heads], rsum[:, n, 0:heads], esk, ALU.add))
                    step(V.reciprocal(rinv[:, n, 0:heads], rsum[:, n, 0:heads]))
                bank = acc_job().rearrange("p (h x) -> p h x", h=per)
                finish(n, hq, bank, rinv[:, n, hq * per:(hq + 1) * per].unsqueeze(2).to_broadcast([P, per, hw]))

            for i, (n, h) in enumerate(units):
                T["sc"] += 1
                dve.wait_ge(sc_full, T["sc"])
                bank = scb(T["sc"] - 1)
                if i >= 2:
                    dve.wait_ge(p_ready, T["p"] + i - 1)
                s = sbuf_s[:, i % 2, 0:nk]
                m = masks(n) if masks else None
                if m is None:
                    tell(V.tensor_copy(s, bank[:, 0:nk]), sc_free)
                elif cq is not None:
                    tell(stt(s, bank[:, 0:nk], cq(n, h), m, ALU.subtract, ALU.add), sc_free)
                elif nk == 256:
                    tell(tt(s, bank[:, 0:256], m, ALU.add), sc_free)
                else:
                    step(tt(s[:, 0:256], bank[:, 0:256], m, ALU.add))
                    tell(V.tensor_copy(s[:, 256:nk], bank[:, 256:nk]), sc_free)
                step(V.tensor_reduce(mx[:, 0:1], s, AX, ALU.max))
                if sink:
                    tell(ts(nm[:, n, h:h + 1], mx[:, 0:1], snk[:, h:h + 1], -1.0, ALU.max, ALU.mult), nm_ready)
                else:
                    tell(ts(nm[:, n, h:h + 1], mx[:, 0:1], -1.0, None, ALU.mult), nm_ready)
                if h == heads - 1:
                    dve.wait_ge(p_ready, T["p"] + i + 1)
                    for hq in range(heads // per):
                        close(n, hq)
            T["p"] += len(units)

        def layer_norm(nt, src, width):
            for t in range(nt):
                for c in range(0, width, 512):
                    k = c // 512
                    step(V.bn_stats(bst[:, 6 * k:6 * k + 6], src(t)[:, c:min(width, c + 512)]))
                step(V.bn_aggr(mv[:, t, :], bst[:, 0:6 * ((width + 511) // 512)]))
            by_act(ts(rstd[:, 0:nt], mv[:, 0:nt, 1], EPS, None, ALU.add))
            step(V.reciprocal(rstd[:, 0:nt], rstd[:, 0:nt]))

        def norm_affine(nt):
            layer_norm(nt, lambda t: S[:, t, :], D)
            for t in range(nt):
                go(ts(S[:, t, :], S[:, t, :], mv[:, t, 0:1], rstd[:, t:t + 1], ALU.subtract, ALU.mult))
            done()
            for k, op in ((0, ALU.mult), (1, ALU.add)):
                for t in range(nt):
                    go(tt(S[:, t, :], S[:, t, :], lnB[:, k, :], op))
                done()

        def rms(src, scratch):
            for t in range(NX):
                step(tt(scratch(t), src(t), src(t), ALU.mult))
                step(V.tensor_reduce(rstd[:, t:t + 1], scratch(t), AX, ALU.add))
            by_act(ts(rstd[:, 0:NX], rstd[:, 0:NX], 1.0 / D, EPS, ALU.mult, ALU.add))
            step(V.reciprocal(rstd[:, 0:NX], rstd[:, 0:NX]))

        def leave():
            by_act()
            dve.sem_inc(phase, 1)
            T["phase"] += 2
            dve.wait_ge(phase, T["phase"])

        def modulate(nt, s):
            for t in range(nt):
                r = 2 * (t // 2)
                step(stt(hb[:, t, :], modB[:, r + 1, :], 1.0, S[:, t, :], ALU.add, ALU.mult))
                tell(tt(hb[:, t, :], hb[:, t, :], modB[:, r, :], ALU.add), s)

        step(V.memset(mx[:, :], 0.0))
        step(V.memset(small[:, 1023:1024], 0.0))
        dve.wait_ge(c_exp, 1)
        step(ts(ce, ce, 1.0, None, ALU.add))
        step(V.reciprocal(ce, ce))
        step(tt(ce, cact[:, :, :], ce, ALU.mult))
        tell(V.tensor_copy(cact32[:, :, :].rearrange("p c (r i) -> p c r i", i=2),
                           ce.unsqueeze(2).to_broadcast([P, DC, 16, 2])), c_ready)
        dve.wait_ge(const_in, 48)
        for l in range(DEPTH):
            nt = 4 if l < DEPTH - 1 else NX
            dve.wait_ge(bada_in, 16 * (5 + 4 * l))
            for j in range(ADA_TILES):
                bank = acc_job()
                read(tt(mst[:, j, :], bank[:, 0:P], mst[:, j, :], ALU.add))
                if j % 6 == 5:
                    tell(V.tensor_copy(mx[0:1, 1:2], mx[0:1, 0:1]), rows_ready)
            T["mod"] += 16 * 4
            dve.wait_ge(mod_in, T["mod"])
            modulate(4, h_ready)
            tell(V.tensor_copy(mx[0:1, 1:2], mx[0:1, 0:1]), mod_used)
            for t in range(nt):
                bank = acc_job()
                q3 = hb[:, t, 0:512].rearrange("p (h x) -> p h x", h=NH)
                if t < NX:
                    step(rope(q3, bank, NH, "ropeA", t, 2))
                else:
                    read(V.tensor_copy(hb[:, t, 0:512], bank))
            for t in range(4):
                bank = acc_job()
                kd = hb[:, t, 512:768].rearrange("p (h b x) -> p h b x", h=NKV, b=2)
                step(V.tensor_copy(vA[:, t, :], bank[:, 128:256]))
                if t < nt:
                    step(V.tensor_copy(guv[:, t, 0:256], bank[:, 256:512]))
                if t < NX:
                    step(rope(kd[:, :, 0, :], bank[:, 0:128], NKV, "ropeA", t, 2))
                else:
                    read(V.tensor_copy(kd[:, :, 0, :], bank[:, 0:128].rearrange("p (h x) -> p h x", h=NKV)))
                step(V.tensor_copy(kd[:, :, 1, :], kd[:, :, 0, :]))
            for t in range(nt):
                bank = acc_job()
                read(V.tensor_copy(guv[:, t, 256:512], bank[:, 0:256]))
            for m in range(2):
                bank = acc_job()
                read(V.tensor_copy(cbT[:, m, 0:nt * P], bank[:, 0:nt * P]))
            nseg = nt // 2
            step(V.memset(uT[:, :, :, :], 0.0))
            for m in range(2):
                bank = acc_job()
                read(V.tensor_copy(ccT[:, 0:nt * P], bank[:, 0:nt * P]))
                bank = acc_job()
                read(tt(uT[:, m, 0:nseg, 1:257], bank[:, 0:nt * P].rearrange("p (s x) -> p s x", s=nseg),
                        ccT[:, 0:nt * P].rearrange("p (s x) -> p s x", s=nseg), ALU.mult))
            for t in range(4):
                tell(V.tensor_copy(mx[:, 1:2], mx[:, 0:1]), qk_ready)
            by_act()
            layer_norm(nt, lambda t: guv[:, t, 256:512], 256)
            for t in range(nt):
                ins = ts(guv[:, t, 256:512], guv[:, t, 256:512], mv[:, t, 0:1], rstd[:, t:t + 1],
                         ALU.subtract, ALU.mult)
                step(ins)
            dve.wait_ge(par_in, par_a(l, 6))
            tell(V.tensor_copy(mx[:, 1:2], mx[:, 0:1]), v_ready)
            for t in range(nt):
                bank = acc_job()
                for q in range(4):
                    c = slice(q * 64, (q + 1) * 64)
                    ins = stt(hb[:, t, 768 + q * 64:768 + (q + 1) * 64], bank[:, c], gmb[:, q:q + 1],
                              guv[:, t, c], ALU.add, ALU.mult)
                    read(ins) if q == 3 else step(ins)

            def put_rows(n, hq, bank, inv):
                read(tt(hb[:, n, 0:512].rearrange("p (h x) -> p h x", h=NH), bank, inv, ALU.mult))
                tell(V.tensor_copy(mx[:, 1:2], mx[:, 0:1]), h_ready)

            attention([(n, h) for n in range(NX) for h in range(NH)], 512,
                      lambda n: const("z1", 256) if n == 0 else const("ge", 256),
                      None, True, NH, HD, put_rows)
            if nt == 4:
                attention([(n, h) for n in range(NX, 4) for h in range(NH)], 256, None, None, True, NH, HD,
                          put_rows)
            for m in range(2):
                for s in range(nseg):
                    y = hT8[:, 4 + m, s * 256:(s + 1) * 256]
                    step(ts(y, uT[:, m, s, 0:256], cwA[:, m, 0:1], None, ALU.mult))
                    step(stt(y, uT[:, m, s, 1:257], cwA[:, m, 1:2], y, ALU.mult, ALU.add))
                    step(stt(y, uT[:, m, s, 2:258], cwA[:, m, 2:3], y, ALU.mult, ALU.add))
                    step(tt(y, y, cbT[:, m, s * 256:(s + 1) * 256], ALU.mult))
            tell(V.tensor_copy(mx[:, 1:2], mx[:, 0:1]), v_ready)
            T["mod"] += 16 * (nt // 2)
            dve.wait_ge(mod_in, T["mod"])
            for j in range(OUT_TILES):
                c = slice(j * 512, (j + 1) * 512)
                for t in range(nt):
                    bank = acc_job()
                    read(tt(hb[:, t, c], bank, modB[:, t // 2, c], ALU.mult))
                    step(stt(S[:, t, c], S[:, t, c], ALPHA, hb[:, t, c], ALU.mult, ALU.add))
            norm_affine(nt)
            tell(V.tensor_copy(mx[:, 1:2], mx[:, 0:1]), mod_used)
            leave()

            T["mod"] += 16 * 2 * (nt // 2)
            dve.wait_ge(mod_in, T["mod"])
            for t in range(nt):
                r = 2 * (t // 2)
                step(stt(hb[:, t, :], modB[:, r + 1, :], 1.0, S[:, t, :], ALU.add, ALU.mult))
                step(tt(hb[:, t, :], hb[:, t, :], modB[:, r, :], ALU.add))
                tell(V.tensor_copy(mx[:, 1:2], mx[:, 0:1]), h_ready)
                tell(V.tensor_copy(mx[:, 1:2], mx[:, 0:1]), tok_ready)
            tell(V.tensor_copy(mx[:, 1:2], mx[:, 0:1]), mod_used)
            dve.wait_ge(par_in, par_a(l, 10))
            for t in range(nt):
                bank = acc_job()
                read(tt(lg[:, t, :], bank[:, 0:36], rb, ALU.add))

            def bc(v, n):
                return v[:, 0:nt].unsqueeze(2).to_broadcast([P, nt, n])

            def io(n, off=0):
                return iota[:, off:off + n].unsqueeze(1).to_broadcast([P, nt, n])

            def first_max(out, val, m, tmp, tmp1, n):
                step(V.tensor_reduce(m[:, 0:nt], val, AX, ALU.max))
                step(tt(tmp, val, bc(m, n), ALU.is_equal))
                step(ts(tmp, tmp, -64.0, None, ALU.mult))
                step(tt(tmp, tmp, io(n), ALU.add))
                step(V.tensor_reduce(tmp1[:, 0:nt], tmp, AX, ALU.min))
                step(tt(out, tmp, bc(tmp1, n), ALU.is_equal))

            gl = lg[:, 0:nt, 0:4]
            ohg = g4[1][:, 0:nt, :]
            first_max(ohg, gl, rt[0], g4[2][:, 0:nt, :], rt[1], NG)
            by_act(tt(g4[0][:, 0:nt, :], gl, bc(rt[0], NG), ALU.subtract))
            step(V.tensor_reduce(rt[3][:, 0:nt], g4[0][:, 0:nt, :], AX, ALU.add))
            step(V.reciprocal(rt[3][:, 0:nt], rt[3][:, 0:nt]))
            step(ts(g4[2][:, 0:nt, :], ohg, 1e30, -1e30, ALU.mult, ALU.add))
            for t in range(nt):
                step(tt(em[:, t, :].rearrange("p (g e) -> p g e", g=NG),
                        lg[:, t, 4:36].rearrange("p (g e) -> p g e", g=NG),
                        g4[2][:, t, :].unsqueeze(2).to_broadcast([P, NG, EPG]), ALU.add))
            emv, ta, tb = em[:, 0:nt, :], t32[0][:, 0:nt, :], t32[1][:, 0:nt, :]
            oh1, oh2 = oh[0][:, 0:nt, :], oh[1][:, 0:nt, :]
            first_max(oh1, emv, rt[0], ta, rt[1], E)
            step(ts(ta, oh1, -2e30, None, ALU.mult))
            step(tt(emv, emv, ta, ALU.add))
            first_max(oh2, emv, rt[2], ta, rt[1], E)
            by_act(tt(rt[2][:, 0:nt], rt[2][:, 0:nt], rt[0][:, 0:nt], ALU.subtract))
            step(ts(rt[4][:, 0:nt], rt[2][:, 0:nt], 1.0, None, ALU.add))
            step(V.reciprocal(rt[4][:, 0:nt], rt[4][:, 0:nt]))
            step(tt(gates[:, 0, 0:nt], rt[4][:, 0:nt], rt[3][:, 0:nt], ALU.mult))
            step(tt(gates[:, 1, 0:nt], gates[:, 0, 0:nt], rt[2][:, 0:nt], ALU.mult))
            tell(tt(mem_[:, 0:nt, :], oh1, oh2, ALU.add), v_ready)
            bank = acc_job()
            step(V.tensor_copy(rk[:, 0:nt * E], bank[:, 0:nt * E]))
            read(V.tensor_copy(rk[:, 4 * E:5 * E], bank[:, 4 * E:5 * E]))
            cnt = rk[:, 4 * E:5 * E]
            step(ts(nov, cnt, float(P + 1), None, ALU.is_ge))
            for m in (2, 3):
                step(ts(sc0, cnt, float(m * P + 1), None, ALU.is_ge))
                step(tt(nov, nov, sc0, ALU.add))
            step(ts(sc0, cnt, 65.0, None, ALU.is_ge))
            step(V.tensor_copy(wide[:, :], sc0))
            step(ts(nar, sc0, -1.0, 1.0, ALU.mult, ALU.add))
            step(V.tensor_copy(sc0, nov))
            a, b = sc0, sc1
            k = 1
            while k < E:
                step(V.tensor_copy(b[:, 0:k], a[:, 0:k]))
                step(tt(b[:, k:E], a[:, k:E], a[:, 0:E - k], ALU.add))
                a, b = b, a
                k *= 2
            step(tt(ovx, a, nov, ALU.subtract))
            no = 8
            jb = iota[:, 0:no].unsqueeze(2).to_broadcast([P, no, E])
            step(tt(ov3, ovx.unsqueeze(1).to_broadcast([P, no, E]), jb, ALU.is_le))
            step(tt(ov4, a.unsqueeze(1).to_broadcast([P, no, E]), jb, ALU.is_gt))
            step(tt(ov3, ov3, ov4, ALU.mult))
            step(tt(ov3, ov3, iota[:, 0:E].unsqueeze(1).to_broadcast([P, no, E]), ALU.mult))
            step(V.tensor_reduce(ov1, ov3, AX, ALU.add))
            step(V.tensor_copy(ovid[:, 0:8], ov1))
            step(V.tensor_copy(ovid[:, 8:9], a[:, E - 1:E]))
            rkv = rk[:, 0:nt * E].rearrange("p (t e) -> p t e", t=nt)
            nb = E + OVERFLOW[l]
            for k, o in enumerate((oh1, oh2)):
                r, q, e, x, w_ = (rt[5][:, 0:nt], rt[6][:, 0:nt], rt[7][:, 0:nt], rt[8][:, 0:nt], rt[9][:, 0:nt])
                step(tt(ta, rkv, o, ALU.mult))
                step(V.tensor_reduce(r, ta, AX, ALU.add))
                step(tt(ta, io(E), o, ALU.mult))
                step(V.tensor_reduce(e, ta, AX, ALU.add))
                step(tt(ta, ovx.unsqueeze(1).to_broadcast([P, nt, E]), o, ALU.mult))
                step(V.tensor_reduce(x, ta, AX, ALU.add))
                step(ts(q, r, float(P), None, ALU.is_ge))
                for m in (2, 3):
                    step(ts(w_, r, float(m * P), None, ALU.is_ge))
                    step(tt(q, q, w_, ALU.add))
                step(stt(r, q, -float(P), r, ALU.mult, ALU.add))
                step(tt(x, x, q, ALU.add))
                step(ts(x, x, float(E - 1), None, ALU.add))
                step(tt(x, x, e, ALU.subtract))
                step(ts(q, q, 1.0, None, ALU.min))
                step(tt(x, x, q, ALU.mult))
                step(tt(x, x, e, ALU.add))
                step(stt(w_, x, float(P), r, ALU.mult, ALU.add))
                step(ts(w_, w_, 2.0, None, ALU.mult))
                step(V.tensor_copy(dest[:, 0:nt, k, 0], w_))
                step(tt(ta, nar.unsqueeze(1).to_broadcast([P, nt, E]), o, ALU.mult))
                step(V.tensor_reduce(q, ta, AX, ALU.add))
                step(stt(w_, q, 128.0, w_, ALU.mult, ALU.add))
                step(ts(w_, w_, 1.0, None, ALU.add))
                step(V.tensor_copy(dest[:, 0:nt, k, 1], w_))
                step(tt(R[k][:, 0:nt, :], io(P), bc(rt[5], P), ALU.is_equal))
                step(tt(bo[k][:, 0:nt, 0:nb], io(nb), bc(rt[8], nb), ALU.is_equal))
                step(tt(bo[k][:, 0:nt, 0:nb], bo[k][:, 0:nt, 0:nb],
                        const("tokid", nt).unsqueeze(2).to_broadcast([P, nt, nb]), ALU.mult))
            tell(V.tensor_copy(mx[:, 1:2], mx[:, 0:1]), v_ready)
            bank = acc_job()
            read(V.tensor_copy(slot_tok[:, 0:nb], bank[:, 0:nb]))
            tell(V.tensor_copy(mx[:, 1:2], mx[:, 0:1]), idx_ready)
            B0 = blocks_before[l]
            with dve.Fori(0, E // UNROLL) as i:
                for u in range(UNROLL):
                    p = u % 2
                    b = i * UNROLL + (B0 + u)
                    dve.wait_ge(m_e, b + 1)
                    dve.wait_ge(m_h3, b + 1)
                    tt(gbuf[:, p, :], ps[:, 2 + p, :], eb[:, p, :], ALU.mult).then_inc(m_g, 1)
                    dve.wait_ge(m_y, b + 1)
                    dve.wait_ge(m_yw[p], i * 32 + 16 * ((B0 + u) // 2 + 1))
                    V.tensor_copy(ysb[:, p, :].rearrange("p (n x) -> p n x", n=2), ps[:, 6:8, :]).then_inc(m_ye, 1)
            o = ov[l]
            n_over = dve.value_load(ovid[0:1, 8:9], min_val=0, max_val=8)
            with dve.If(n_over > 0):
                with dve.Fori(0, OVERFLOW[l]) as j:
                    dve.wait_ge(o["silu"], j + 1)
                    tt(gbuf[:, 0, :], ps[:, 2, :], eb[:, 0, :], ALU.mult).then_inc(o["gated"], 1)
                    dve.wait_ge(o["y"], j + 1)
                    V.tensor_copy(ysb[:, 0, :].rearrange("p (n x) -> p n x", n=2),
                                  ps[:, 6:8, :]).then_inc(o["y_copied"], 1)
            T["mod"] += 16 * (nt // 2)
            dve.wait_ge(mod_in, T["mod"])
            for t in range(nt):
                T["cin", t % 2] += 64
                dve.wait_ge(comb_in[t % 2], T["cin", t % 2])
                y0, y1 = yg[0][:, t % 2, :], yg[1][:, t % 2, :]
                step(ts(y0, y0, gates[:, 0, t:t + 1], None, ALU.mult))
                step(stt(y0, y1, gates[:, 1, t:t + 1], y0, ALU.mult, ALU.add))
                step(tt(y0, y0, modB[:, t // 2, :], ALU.mult))
                ins = stt(S[:, t, :], S[:, t, :], ALPHA, y0, ALU.mult, ALU.add)
                if t < nt - 2:
                    tell(ins, comb_used)
                else:
                    step(ins)
            norm_affine(nt)
            leave()

        for l in range(DEPTH):
            dve.wait_ge(par_in, par_b(l, 9))
            rms(lambda t: S[:, t, :], lambda t: hb[:, t, :])
            for t in range(NX):
                step(ts(hB[:, t, :], S[:, t, :], rstd[:, t:t + 1], None, ALU.mult))
                tell(tt(hB[:, t, :], hB[:, t, :], lnB[:, 0, :], ALU.mult), h_ready)
            for t in range(NX):
                bank = acc_job()
                step(rope(mixB[:, t, 0:512].rearrange("p (h x) -> p h x", h=NH), bank, NH, "ropeB", t, 1))
            for t in range(NX):
                bank = acc_job()
                kd = mixB[:, t, 512:768].rearrange("p (h b x) -> p h b x", h=NKV, b=2)
                step(V.tensor_copy(vaB[:, t, :], bank[:, 128:256]))
                step(V.tensor_copy(fbd[:, t, :], bank[:, 256:280]))
                step(rope(kd[:, :, 0, :], bank[:, 0:128], NKV, "ropeB", t, 1))
                step(V.tensor_copy(kd[:, :, 1, :], kd[:, :, 0, :]))
            for t in range(NX):
                bank = acc_job()
                read(V.tensor_copy(gaB[:, t, :], bank))
            for m in range(2):
                bank = acc_job()
                read(ts(qbT[:, 2 * m:2 * m + 2, :], bank.rearrange("p (a b) -> p a b", a=2), QSCALE, None, ALU.mult))
            for m in range(2):
                bank = acc_job()
                read(V.tensor_copy(kbT[:, 2 * m:2 * m + 2, :], bank.rearrange("p (a b) -> p a b", a=2)))
            for t in range(NX):
                bank = acc_job()
                read(V.tensor_copy(vbB[:, t, :], bank))
            for t in range(NX):
                bank = acc_job()
                read(V.tensor_copy(gbB[:, t, :], bank))
            for j in range(2):
                for t in range(NX):
                    bank = acc_job()
                    read(V.tensor_copy(zB[:, t, j * 512:(j + 1) * 512], bank))
            step(V.memset(xp[:, :, 0:3], 0.0))
            for m in range(6):
                bank = acc_job()
                read(V.tensor_copy(xp[:, 2 * m:2 * m + 2, 3:259], bank.rearrange("p (a b) -> p a b", a=2)))
            for t in range(NX):
                tell(V.tensor_copy(mx[:, 1:2], mx[:, 0:1]), qk_ready)
            V.tensor_copy(mx[:, 1:2], mx[:, 0:1]).then_inc(dve_to_act, 1)
            for k in (3, 0, 1, 2):
                for c in range(12):
                    y = xc[:, c, :]
                    if k == 3:
                        go(ts(y, xp[:, c, 3:259], cwB[:, c, 3:4], cbB[:, c:c + 1], ALU.mult, ALU.add))
                    else:
                        go(stt(y, xp[:, c, k:k + 256], cwB[:, c, k:k + 1], y, ALU.mult, ALU.add))
                done()
            T["a2d"] += 1
            dve.wait_ge(act_to_dve, T["a2d"])
            by_act()
            v, e_, z_, o_ = sp
            for t in range(NX):
                step(tt(v[:, t, :], fbd[:, t, :], bfd, ALU.add))
            step(ts(v[:, :, 0:8], v[:, :, 0:8], -1.0, None, ALU.mult))
            step(ts(e_, v, -1.0, None, ALU.mult))
            by_act(tt(e_, e_, v, ALU.max))
            step(ts(z_, e_, 2.0, None, ALU.add))
            step(V.reciprocal(z_, z_))
            step(tt(z_, z_, e_, ALU.mult))
            step(tt(e_, z_, z_, ALU.mult))
            step(ts(o_, e_, 1.0 / 17, 1.0 / 15, ALU.mult, ALU.add))
            for k in (13, 11, 9, 7, 5, 3, 1):
                step(tt(o_, o_, e_, ALU.mult))
                step(ts(o_, o_, 1.0 / k, None, ALU.add))
            step(tt(o_, o_, z_, ALU.mult))
            step(ts(v, v, 0.0, None, ALU.max))
            step(ts(o_, o_, 2.0, None, ALU.mult))
            step(tt(o_, o_, v, ALU.add))
            by_act()
            for t in range(NX):
                step(tt(dta[:, t, :], o_[:, t, 8:24], aneg, ALU.mult))
            step(ts(dta, dta, -1.0, None, ALU.mult))

            def put_a(n, hq, bank, inv):
                out = mixB[:, n, 0:512].rearrange("p (h x) -> p h x", h=NH)
                read(tt(out, bank, inv, ALU.mult))
                step(tt(mixB[:, n, 0:512], mixB[:, n, 0:512], gaB[:, n, :], ALU.mult))

            attention([(n, h) for n in range(NX) for h in range(NH)], 256,
                      lambda n: const("causal", 256) if n == 0 else const("gt", 256),
                      None, True, NH, HD, put_a)
            tell(V.tensor_copy(mx[:, 1:2], mx[:, 0:1]), v_ready)
            bank = acc_job()
            read(V.tensor_copy(cs, bank[:, 0:80]))

            def put_b(n, hq, bank, inv):
                out = mixB[:, n, 512:1024].rearrange("p (h x) -> p h x", h=NH)
                read(tt(out, bank, inv, ALU.mult))
                step(tt(mixB[:, n, 512:1024], mixB[:, n, 512:1024], gbB[:, n, :], ALU.mult))

            attention([(n, h) for n in range(NX) for h in range(NH)], 256,
                      lambda n: const("causal", 256) if n == 0 else const("z1", 256),
                      lambda n, h: cs[:, 64 + 8 * n + h:65 + 8 * n + h], False, NH, HD, put_b)
            dtv = o_[:, :, 8:24]
            for t in range(NX):
                bank = acc_job()
                read(V.tensor_copy(cbm[:, t, :, :], bank[:, 0:256].rearrange("p (g l) -> p g l", g=2)))
            by_act(tt(dst, cs[:, 32:48], cs[:, 0:16], ALU.subtract))
            by_act()
            for t in range(NX):
                step(tt(xdt[:, t, :].rearrange("p (h x) -> p h x", h=16),
                        xsn[:, t, :].rearrange("p (h x) -> p h x", h=16),
                        dtv[:, t, :].unsqueeze(2).to_broadcast([P, 16, HD]), ALU.mult))
            tell(tt(xds.rearrange("p (h x) -> p h x", h=16), xdt[:, 0, :].rearrange("p (h x) -> p h x", h=16),
                    dst.unsqueeze(2).to_broadcast([P, 16, HD]), ALU.mult), v_ready)
            for q in range(2):
                bank = acc_job()
                read(V.tensor_copy(stT[:, q, :], bank))
            tell(V.tensor_copy(mx[:, 1:2], mx[:, 0:1]), v_ready)
            for i in range(8):
                t, q4 = i // 4, i % 4
                T["sc"] += 1
                dve.wait_ge(sc_full, T["sc"])
                bank = scb(T["sc"] - 1).rearrange("p (h l) -> p h l", h=4)
                w3 = W[:, i % 2, :].rearrange("p (h l) -> p h l", h=4)
                acs = cs[:, 16 * t + 4 * q4:16 * t + 4 * q4 + 4].unsqueeze(2).to_broadcast([P, 4, P])
                tell(tt(w3, bank, acs, ALU.subtract), sc_free)
                by_act(tt(w3, w3, const("ge").unsqueeze(1).to_broadcast([P, 4, P]), ALU.add))
                tell(tt(W2[:, i % 2, :].rearrange("p (h l) -> p h l", h=4), w3,
                        cbm[:, t, q4 // 2, :].unsqueeze(1).to_broadcast([P, 4, P]), ALU.mult), w_ready)
                if q4 % 2 == 1:
                    q = q4 // 2
                    c = slice(1024 + q * 512, 1536 + q * 512)
                    bank = acc_job()
                    y3 = mixB[:, t, c].rearrange("p (h x) -> p h x", h=8)
                    xs3 = xsn[:, t, q * 512:(q + 1) * 512].rearrange("p (h x) -> p h x", h=8)
                    step(tt(y3, xs3, dskip[:, 8 * q:8 * q + 8].unsqueeze(2).to_broadcast([P, 8, HD]), ALU.mult))
                    read(tt(mixB[:, t, c], bank, mixB[:, t, c], ALU.add))
                    if t == 1:
                        bank = acc_job()
                        tmp3 = lnB[:, 0, 0:512].rearrange("p (h x) -> p h x", h=8)
                        read(tt(tmp3, bank.rearrange("p (h x) -> p h x", h=8),
                                eacs[:, 8 * q:8 * q + 8].unsqueeze(2).to_broadcast([P, 8, HD]), ALU.mult))
                        step(tt(mixB[:, t, c], mixB[:, t, c], lnB[:, 0, 0:512], ALU.add))
            for t in range(NX):
                step(tt(mixB[:, t, 1024:2048], mixB[:, t, 1024:2048], zB[:, t, :], ALU.mult))
            rms(lambda t: mixB[:, t, 1024:2048], lambda t: lnB[:, 0, :])
            for t in range(NX):
                y = mixB[:, t, 1024:2048]
                step(ts(y, y, rstd[:, t:t + 1], None, ALU.mult))
                tell(tt(y, y, lnB[:, 1, :], ALU.mult), h_ready)
            for n in range(2):
                for t in range(NX):
                    bank = acc_job()
                    c = slice(n * 512, (n + 1) * 512)
                    read(tt(S[:, t, c], bank, S[:, t, c], ALU.add))
            leave()
            dve.wait_ge(par_in, par_b(l, 12))
            rms(lambda t: memn[:, t, :], lambda t: hb[:, t, :])
            for t in range(NX):
                step(ts(memn[:, t, :], memn[:, t, :], rstd[:, t:t + 1], None, ALU.mult))
                tell(tt(memn[:, t, :], memn[:, t, :], lnB[:, 1, :], ALU.mult), h_ready)
            rms(lambda t: S[:, t, :], lambda t: hb[:, t, :])
            for t in range(NX):
                step(ts(hB[:, t, :], S[:, t, :], rstd[:, t:t + 1], None, ALU.mult))
                tell(tt(hB[:, t, :], hB[:, t, :], lnB[:, 0, :], ALU.mult), h_ready)
            for m in range(4):
                bank = acc_job()
                read(V.tensor_copy(kmT[:, 2 * m:2 * m + 2, :], bank.rearrange("p (a b) -> p a b", a=2)))
            for j in range(2):
                for t in range(NX):
                    bank = acc_job()
                    read(V.tensor_copy(vm[:, t, j * 512:(j + 1) * 512], bank))
            for m in range(4):
                bank = acc_job()
                read(ts(qmT[:, 2 * m:2 * m + 2, :], bank.rearrange("p (a b) -> p a b", a=2), MEM_QSCALE, None,
                        ALU.mult))
            tell(V.tensor_copy(mx[:, 1:2], mx[:, 0:1]), v_ready)

            def put_m(n, hq, bank, inv):
                out = mixB[:, n, hq * 512:(hq + 1) * 512].rearrange("p (h x) -> p h x", h=2)
                read(tt(out, bank, inv, ALU.mult))
                if hq == 1:
                    tell(V.tensor_copy(mx[:, 1:2], mx[:, 0:1]), h_ready)

            attention([(n, h) for n in range(NX) for h in range(4)], 256, None, None, False, 4, 256, put_m)
            for n in range(2):
                for t in range(NX):
                    bank = acc_job()
                    c = slice(n * 512, (n + 1) * 512)
                    read(tt(S[:, t, c], bank, S[:, t, c], ALU.add))
            leave()
        dve.wait_ge(par_in, par_b(DEPTH, 1))
        rms(lambda t: S[:, t, :], lambda t: hb[:, t, :])
        for t in range(NX):
            step(ts(hb[:, t, :], S[:, t, :], rstd[:, t:t + 1], None, ALU.mult))
            step(tt(hb[:, t, :], hb[:, t, :], lnB[:, 0, :], ALU.mult))
        tell(V.tensor_copy(mx[:, 1:2], mx[:, 0:1]), out_ready)


def _tile(w):
    out = np.zeros((P, DC, 512), w.dtype)
    out[:, :, :w.shape[1]] = w.reshape(DC, P, -1).transpose(1, 0, 2)
    return out.reshape(P, TILE)


def _cols(w, n=512):
    return [_tile(w[:, i:i + n]) for i in range(0, w.shape[1], n)]


def _layout(a):
    o = {"consts": constants()}
    o["x"], o["ctx"], o["mem_2"] = a["x"][0], a["ctx"][0], a["mem_2"][0]
    o["cpack"] = np.stack([a["c"][0].reshape(DC, P).T, a["c_ctx"].reshape(DC, P).T], 2).reshape(P, 2 * DC)
    dA, dB, moe = [], [], []
    for l in range(DEPTH):
        w = a["w_in"][l]
        dA.append(np.stack(
            _cols(a["w_ada"][l])
            + [_tile(w[:, 0:512]), _tile(np.concatenate([w[:, 512:768], w[:, 1536:1792]], 1)),
               _tile(np.concatenate([w[:, 1792:2048], w[:, 768:1024]], 1)), _tile(w[:, 1024:1536])]
            + _cols(a["w_out"][l])))
        w = a["w_in_2"][l]
        o2 = a["w_out_2"][l]
        dB.append(np.stack(
            [_tile(w[:, 0:512]), _tile(np.concatenate([w[:, 512:768], w[:, 2816:2824], w[:, 5896:5912]], 1)),
             _tile(w[:, 768:1280]), _tile(w[:, 1280:1792]), _tile(w[:, 1792:2304]), _tile(w[:, 2304:2816]),
             _tile(w[:, 2824:3336]), _tile(w[:, 3336:3848]), _tile(w[:, 3848:4360]), _tile(w[:, 4360:4872]),
             _tile(w[:, 4872:5384]), _tile(w[:, 5384:5896])]
            + [_tile(o2[k * D:(k + 1) * D, n * 512:(n + 1) * 512]) for n in range(2) for k in range(2)]
            + _cols(a["w_mk_2"][l]) + _cols(a["w_mv_2"][l]) + _cols(a["w_mq_2"][l]) + _cols(a["w_mo_2"][l])))
    o["denseA"], o["denseB"] = np.stack(dA), np.stack(dB)
    moe = np.empty((DEPTH, E, 3, P, TILE), np.float32)
    for k, n in enumerate(("w1", "w3")):
        moe[:, :, k] = a[n].reshape(DEPTH, E, DC, P, 512).transpose(0, 1, 3, 2, 4).reshape(DEPTH, E, P, TILE)
    moe[:, :, 2] = a["w2"].reshape(DEPTH, E, 4, P, D).transpose(0, 1, 3, 2, 4).reshape(DEPTH, E, P, TILE)
    o["moe"] = moe.reshape(DEPTH, 3 * E, P, TILE)
    for n in ("b_ada", "attn_sink", "ln1_g", "ln1_b", "ln2_g", "ln2_b", "norm_mix_w_2", "ssm_norm_w_2",
              "swa_sinks_2", "b_forget_2", "dt_bias_2", "a_log_2", "d_skip_2", "norm_xq_w_2", "norm_mem_w_2",
              "final_norm_w_2"):
        o[n] = a[n]
    o["gm_ws"] = a["gm_ws"].transpose(0, 3, 1, 2).reshape(DEPTH, P, 4 * P)
    o["gm_bs"] = a["gm_bs"].transpose(0, 2, 1)
    o["conv_w"] = a["conv_w"].reshape(DEPTH, 3, 2, P).transpose(0, 3, 2, 1).reshape(DEPTH, P, 6)
    o["conv_w_2"] = a["conv_w_2"].reshape(DEPTH, 4, 12, P).transpose(0, 3, 2, 1).reshape(DEPTH, P, 48)
    o["conv_b_2"] = a["conv_b_2"].reshape(DEPTH, 12, P).transpose(0, 2, 1)
    wr = np.concatenate([a["w_rg"], a["w_re"]], 2)
    o["w_route"] = wr.reshape(DEPTH, DC, P, 36).transpose(0, 2, 1, 3).reshape(DEPTH, P, DC * 36)
    o["b_route"] = np.concatenate([a["b_rg"], a["b_re"]], 1)
    return o


def kernel(**inputs):
    import concourse.bacc as _bacc
    from concourse.bass_utils import run_bass_kernel_spmd as _run

    nc = _bacc.Bacc("TRN2", target_bir_lowering=False, num_devices=1)
    arrays, d = {}, {}
    for name, v in _layout({k: np.asarray(v) for k, v in inputs.items()}).items():
        v = np.ascontiguousarray(v)
        arrays[f"in_{name}"] = v
        d[name] = nc.dram_tensor(f"in_{name}", v.shape, mybir.dt.from_np(v.dtype), kind="ExternalInput").ap()
    d["out"] = nc.dram_tensor("out_0", (NX * P, D), F32, kind="ExternalOutput").ap()
    build(nc, d)
    r = _run(nc, [arrays], core_ids=[0])
    return r.results[0]["out_0"].reshape(1, NX * P, D)
```
